# Optimizing a Trainium2 kernel written in Bass

```python
import jax
import jax.numpy as jnp
from jax import lax
import numpy as np
import math
import jax, jax.numpy as jnp

D_MODEL = 1024
BATCH = 1
SEQ = 512
DEPTH = 1

CHUNK = 64
D_MLSTM = D_MODEL // 2
D_POOL = D_MODEL - D_MLSTM
N_HEADS = 4
HEAD_DIM = D_MLSTM // N_HEADS
CONV_WIDTH = 4
POOL_WINDOWS = (2, 4, 8, 16)
N_POOL_GROUPS = len(POOL_WINDOWS)
POOL_GROUP_DIM = D_POOL // N_POOL_GROUPS
N_EXPERT_GROUPS = 4
EXPERTS_PER_GROUP = 8
N_EXPERTS = N_EXPERT_GROUPS * EXPERTS_PER_GROUP
TOP_K = 2
D_EXPERT = D_MODEL // 2
MOE_BLOCK = 128
EPS = 1e-6

COL_U = 0
COL_V = COL_U + D_MLSTM
COL_O = COL_V + D_MLSTM
COL_I = COL_O + D_MLSTM
COL_F = COL_I + N_HEADS
COL_P = COL_F + N_HEADS
IN_COLS = COL_P + D_POOL


def rms_norm(x, g):
    xf = x.astype(jnp.float32)
    y = xf * lax.rsqrt(jnp.mean(xf * xf, axis=-1, keepdims=True) + EPS)
    return (y * g.astype(jnp.float32)).astype(x.dtype)

def causal_conv(x, w, b):
    k_w, ch = w.shape
    y = lax.conv_general_dilated(x, w[:, None, :], window_strides=(1,), padding=[(k_w - 1, 0)],
                                 dimension_numbers=('NWC', 'WIO', 'NWC'), feature_group_count=ch)
    return y + b

def mlstm_chunkwise(q, k, v, i_pre, f_pre):
    bsz, nh, seq, dh = q.shape
    nc = seq // CHUNK
    q = q.astype(jnp.float32) * (dh ** -0.5)
    k = k.astype(jnp.float32)
    v = v.astype(jnp.float32)
    log_i = i_pre.astype(jnp.float32)
    log_f = jax.nn.log_sigmoid(f_pre.astype(jnp.float32))

    def to_chunks(a):
        return jnp.moveaxis(a.reshape(bsz, nh, nc, CHUNK, *a.shape[3:]), 2, 0)

    qc, kc, vc, ic = to_chunks(q), to_chunks(k), to_chunks(v), to_chunks(log_i)
    bc = jnp.cumsum(to_chunks(log_f), axis=-1)
    causal = jnp.tril(jnp.ones((CHUNK, CHUNK), dtype=bool))

    def step(carry, inp):
        c_st, n_st, m_st = carry
        q_, k_, v_, ig, b_ = inp
        d_log = b_[..., :, None] - b_[..., None, :] + ig[..., None, :]
        d_log = jnp.where(causal, d_log, -jnp.inf)
        inter = b_ + m_st[..., None]
        m_t = jnp.maximum(inter, jnp.max(d_log, axis=-1))
        w_intra = jnp.exp(d_log - m_t[..., None])
        a_inter = jnp.exp(inter - m_t)
        s = jnp.einsum('bhtd,bhsd->bhts', q_, k_) * w_intra
        num = (a_inter[..., None] * jnp.einsum('bhed,bhtd->bhte', c_st, q_)
               + jnp.einsum('bhts,bhse->bhte', s, v_))
        den = a_inter * jnp.einsum('bhd,bhtd->bht', n_st, q_) + jnp.sum(s, axis=-1)
        h = num / jnp.maximum(jnp.abs(den), jnp.exp(-m_t))[..., None]
        b_last = b_[..., -1]
        w_log = b_last[..., None] - b_ + ig
        m_new = jnp.maximum(b_last + m_st, jnp.max(w_log, axis=-1))
        a_prev = jnp.exp(b_last + m_st - m_new)
        w_s = jnp.exp(w_log - m_new[..., None])
        c_new = a_prev[..., None, None] * c_st + jnp.einsum('bhs,bhse,bhsd->bhed', w_s, v_, k_)
        n_new = a_prev[..., None] * n_st + jnp.einsum('bhs,bhsd->bhd', w_s, k_)
        return (c_new, n_new, m_new), h

    init = (jnp.zeros((bsz, nh, dh, dh), jnp.float32), jnp.zeros((bsz, nh, dh), jnp.float32),
            jnp.zeros((bsz, nh), jnp.float32))
    _, hs = lax.scan(step, init, (qc, kc, vc, ic, bc))
    return jnp.moveaxis(hs, 0, 2).reshape(bsz, nh, seq, dh)

def mlstm_group(u, v, o_pre, i_pre, f_pre, conv_w, conv_b, w_q, w_k, b_i, b_f, norm_g, skip):
    bsz, seq, _ = u.shape
    uc = jax.nn.silu(causal_conv(u, conv_w, conv_b))
    uh = uc.reshape(bsz, seq, N_HEADS, HEAD_DIM)
    q = jnp.einsum('bshd,hde->bhse', uh, w_q)
    k = jnp.einsum('bshd,hde->bhse', uh, w_k)
    vh = v.reshape(bsz, seq, N_HEADS, HEAD_DIM).transpose(0, 2, 1, 3)
    ig = (i_pre + b_i).transpose(0, 2, 1)
    fg = (f_pre + b_f).transpose(0, 2, 1)
    h = mlstm_chunkwise(q, k, vh, ig, fg)
    h = h * lax.rsqrt(jnp.mean(h * h, axis=-1, keepdims=True) + EPS)
    h = h * norm_g.astype(jnp.float32).reshape(N_HEADS, 1, HEAD_DIM)
    h = h.transpose(0, 2, 1, 3).reshape(bsz, seq, D_MLSTM)
    out = jax.nn.sigmoid(o_pre.astype(jnp.float32)) * (h + skip.astype(jnp.float32) * uc.astype(jnp.float32))
    return out.astype(u.dtype)

def pool_group(p, w_pool, b_pool, pool_scale):
    bsz, seq, _ = p.shape
    pf = p.astype(jnp.float32).reshape(bsz, seq, N_POOL_GROUPS, POOL_GROUP_DIM)
    cs = jnp.pad(jnp.cumsum(pf, axis=1), ((0, 0), (1, 0), (0, 0), (0, 0)))
    t = jnp.arange(seq, dtype=jnp.int32)
    win = jnp.array(POOL_WINDOWS, dtype=jnp.int32)
    start = jnp.maximum(t[:, None] + 1 - win[None, :], 0)
    lo = cs[:, start, jnp.arange(N_POOL_GROUPS)[None, :]]
    count = jnp.minimum(t[:, None] + 1, win[None, :]).astype(jnp.float32)
    pooled = (cs[:, 1:] - lo) / count[None, :, :, None] - pf
    y = jnp.einsum('bsgc,gcd->bsgd', pooled, w_pool.astype(jnp.float32)).reshape(bsz, seq, D_POOL)
    y = (y + b_pool.astype(jnp.float32)) * pool_scale.astype(jnp.float32)
    return y.astype(p.dtype)

def hierarchical_moe(h, w_rg, b_rg, w_re, b_re, w_gate, w_up, w_down):
    bsz, seq, dm = h.shape
    n_tok = bsz * seq
    hf = h.reshape(n_tok, dm)
    g_logits = (hf @ w_rg + b_rg).astype(jnp.float32)
    g_prob = jax.nn.softmax(g_logits, axis=-1)
    g_idx = jnp.argmax(g_logits, axis=-1).astype(jnp.int32)
    g_gate = jnp.take_along_axis(g_prob, g_idx[:, None], axis=1)[:, 0]
    e_logits = (hf @ w_re + b_re).astype(jnp.float32).reshape(n_tok, N_EXPERT_GROUPS, EXPERTS_PER_GROUP)
    e_logits = jnp.take_along_axis(e_logits, g_idx[:, None, None], axis=1)[:, 0]
    top_val, top_loc = lax.top_k(e_logits, TOP_K)
    gates = jax.nn.softmax(top_val, axis=-1) * g_gate[:, None]
    expert = g_idx[:, None] * EXPERTS_PER_GROUP + top_loc.astype(jnp.int32)
    n_asg = n_tok * TOP_K
    flat_e = expert.reshape(n_asg)
    flat_tok = jnp.repeat(jnp.arange(n_tok, dtype=jnp.int32), TOP_K)
    flat_gate = gates.reshape(n_asg)
    order = jnp.argsort(flat_e)
    sorted_e = flat_e[order]
    counts = jnp.bincount(flat_e, length=N_EXPERTS).astype(jnp.int32)
    starts = jnp.cumsum(counts) - counts
    padded = (counts + MOE_BLOCK - 1) // MOE_BLOCK * MOE_BLOCK
    pad_ends = jnp.cumsum(padded)
    pad_starts = pad_ends - padded
    rank = jnp.arange(n_asg, dtype=jnp.int32) - starts[sorted_e]
    dest = pad_starts[sorted_e] + rank
    n_blocks = (n_asg + MOE_BLOCK - 1) // MOE_BLOCK + N_EXPERTS
    n_slots = n_blocks * MOE_BLOCK
    slot_tok = jnp.full((n_slots,), n_tok, jnp.int32).at[dest].set(flat_tok[order])
    slot_gate = jnp.zeros((n_slots,), jnp.float32).at[dest].set(flat_gate[order])
    block_pos = jnp.arange(n_blocks, dtype=jnp.int32) * MOE_BLOCK
    block_expert = jnp.minimum(jnp.searchsorted(pad_ends, block_pos, side='right'), N_EXPERTS - 1)

    def run_block(args):
        tok, e = args
        xb = hf[jnp.minimum(tok, n_tok - 1)]
        a = xb @ w_gate[e]
        b = xb @ w_up[e]
        return (jax.nn.silu(a) * b) @ w_down[e]

    out = lax.map(run_block, (slot_tok.reshape(n_blocks, MOE_BLOCK), block_expert))
    out = (out.reshape(n_slots, dm).astype(jnp.float32) * slot_gate[:, None]).astype(h.dtype)
    y = jnp.zeros((n_tok, dm), h.dtype).at[slot_tok].add(out, mode='drop')
    return y.reshape(bsz, seq, dm)

def first_inputs(seed: int = 0) -> dict:
    key = jax.random.key(seed)
    ks = jax.random.split(key, 28)
    L = DEPTH

    def nrm(k, shape, scale):
        return jax.random.normal(k, shape, jnp.float32) * scale

    return {
        'x': nrm(ks[0], (BATCH, SEQ, D_MODEL), 1.0),
        'c': nrm(ks[1], (BATCH, D_MODEL), 1.0),
        'ada_w': nrm(ks[2], (L, D_MODEL, 6 * D_MODEL), D_MODEL ** -0.5),
        'ada_b': nrm(ks[3], (L, 6 * D_MODEL), 0.02),
        'norm1_g': 1.0 + nrm(ks[4], (L, D_MODEL), 0.02),
        'w_in': nrm(ks[5], (L, D_MODEL, IN_COLS), D_MODEL ** -0.5),
        'conv_w': nrm(ks[6], (L, CONV_WIDTH, D_MLSTM), CONV_WIDTH ** -0.5),
        'conv_b': nrm(ks[7], (L, D_MLSTM), 0.02),
        'w_q': nrm(ks[8], (L, N_HEADS, HEAD_DIM, HEAD_DIM), HEAD_DIM ** -0.5),
        'w_k': nrm(ks[9], (L, N_HEADS, HEAD_DIM, HEAD_DIM), HEAD_DIM ** -0.5),
        'b_igate': nrm(ks[10], (L, N_HEADS), 0.1),
        'b_fgate': jnp.linspace(3.0, 6.0, N_HEADS, dtype=jnp.float32)[None, :] + nrm(ks[11], (L, N_HEADS), 0.1),
        'mlstm_norm_g': 1.0 + nrm(ks[12], (L, D_MLSTM), 0.02),
        'mlstm_skip': 1.0 + nrm(ks[13], (L, D_MLSTM), 0.1),
        'w_pool': nrm(ks[14], (L, N_POOL_GROUPS, POOL_GROUP_DIM, POOL_GROUP_DIM), POOL_GROUP_DIM ** -0.5),
        'b_pool': nrm(ks[15], (L, D_POOL), 0.02),
        'pool_scale': 1.0 + nrm(ks[16], (L, D_POOL), 0.1),
        'w_out': nrm(ks[17], (L, D_MODEL, D_MODEL), D_MODEL ** -0.5),
        'norm2_g': 1.0 + nrm(ks[18], (L, D_MODEL), 0.02),
        'w_router_group': nrm(ks[19], (L, D_MODEL, N_EXPERT_GROUPS), D_MODEL ** -0.5),
        'b_router_group': nrm(ks[20], (L, N_EXPERT_GROUPS), 0.01),
        'w_router_expert': nrm(ks[21], (L, D_MODEL, N_EXPERTS), D_MODEL ** -0.5),
        'b_router_expert': nrm(ks[22], (L, N_EXPERTS), 0.01),
        'w_expert_gate': nrm(ks[23], (L, N_EXPERTS, D_MODEL, D_EXPERT), D_MODEL ** -0.5),
        'w_expert_up': nrm(ks[24], (L, N_EXPERTS, D_MODEL, D_EXPERT), D_MODEL ** -0.5),
        'w_expert_down': nrm(ks[25], (L, N_EXPERTS, D_EXPERT, D_MODEL), D_EXPERT ** -0.5),
        'final_g': 1.0 + nrm(ks[26], (D_MODEL,), 0.02),
    }

def first_block(x, c, ada_w, ada_b, norm1_g, w_in, conv_w, conv_b, w_q, w_k, b_igate, b_fgate,
              mlstm_norm_g, mlstm_skip, w_pool, b_pool, pool_scale, w_out, norm2_g,
              w_router_group, b_router_group, w_router_expert, b_router_expert,
              w_expert_gate, w_expert_up, w_expert_down, final_g):
    bsz, seq, dm = x.shape
    for l in range(DEPTH):
        mod = (jax.nn.silu(c) @ ada_w[l] + ada_b[l]).reshape(bsz, 6, dm)
        shift_a, scale_a, gate_a = mod[:, 0, None, :], mod[:, 1, None, :], mod[:, 2, None, :]
        shift_f, scale_f, gate_f = mod[:, 3, None, :], mod[:, 4, None, :], mod[:, 5, None, :]
        h = rms_norm(x, norm1_g[l]) * (1.0 + scale_a) + shift_a
        proj = h @ w_in[l]
        y_m = mlstm_group(proj[..., COL_U:COL_V], proj[..., COL_V:COL_O], proj[..., COL_O:COL_I],
                          proj[..., COL_I:COL_F], proj[..., COL_F:COL_P], conv_w[l], conv_b[l],
                          w_q[l], w_k[l], b_igate[l], b_fgate[l], mlstm_norm_g[l], mlstm_skip[l])
        y_p = pool_group(proj[..., COL_P:IN_COLS], w_pool[l], b_pool[l], pool_scale[l])
        mix = jnp.concatenate([y_m, y_p], axis=-1) @ w_out[l]
        x = x + gate_a * mix
        h = rms_norm(x, norm2_g[l]) * (1.0 + scale_f) + shift_f
        x = x + gate_f * hierarchical_moe(h, w_router_group[l], b_router_group[l], w_router_expert[l],
                                          b_router_expert[l], w_expert_gate[l], w_expert_up[l],
                                          w_expert_down[l])
    return rms_norm(x, final_g)


DEPTH_2 = 2

N_A = DEPTH_2 // 2
N_B = DEPTH_2 - N_A
CHUNK_2 = 128
D_GATE = D_MODEL
N_GROUPS = 8
GROUP_DIM = D_GATE // N_GROUPS
N_HEADS_2 = 8
HEAD_DIM_2 = 64
V_DIM = 2 * HEAD_DIM_2
QK_WIDTH = N_HEADS_2 * 2 * HEAD_DIM_2
V_WIDTH = N_HEADS_2 * V_DIM
Q_BLOCK = 128
D_FF = int(math.ceil(8 * D_MODEL / 3 / 256) * 256)


def _alibi_slopes(n):
    return np.array([2.0 ** (-8.0 * (i + 1) / n) for i in range(n)], dtype=np.float32)

def _lambda_init(layer_idx):
    return 0.8 - 0.6 * math.exp(-0.3 * layer_idx)

def rms_norm_2(x, g):
    xf = x.astype(jnp.float32)
    y = xf * lax.rsqrt(jnp.mean(xf * xf, axis=-1, keepdims=True) + EPS)
    return (y * g.astype(jnp.float32)).astype(x.dtype)

def layer_norm_gain(x, g):
    xf = x.astype(jnp.float32)
    mu = jnp.mean(xf, axis=-1, keepdims=True)
    var = jnp.mean(jnp.square(xf - mu), axis=-1, keepdims=True)
    return ((xf - mu) * lax.rsqrt(var + EPS) * g.astype(jnp.float32)).astype(x.dtype)

def swiglu(h, w_gu, w_down):
    gu = h @ w_gu
    g, u = jnp.split(gu, 2, axis=-1)
    return (jax.nn.silu(g) * u) @ w_down

def gmlp_mixer(h, w_in, v_gain, w_sp, b_sp, w_out):
    B, S, _ = h.shape
    uv = jax.nn.gelu(h @ w_in)
    u, v = jnp.split(uv, 2, axis=-1)
    v = layer_norm_gain(v, v_gain)
    v = v.reshape(B, S // CHUNK_2, CHUNK_2, N_GROUPS, GROUP_DIM)
    causal = jnp.tril(jnp.ones((CHUNK_2, CHUNK_2), dtype=w_sp.dtype))
    z = jnp.einsum('gts,bcsgd->bctgd', w_sp * causal, v)
    z = z + b_sp.T[None, None, :, :, None]
    return (u * z.reshape(B, S, D_GATE)) @ w_out

def shared_kv(x, g, w_kv):
    B, S, _ = x.shape
    kv = rms_norm_2(x, g) @ w_kv
    k = kv[..., :QK_WIDTH].reshape(B, S, N_HEADS_2, 2, HEAD_DIM_2).transpose(0, 2, 3, 1, 4)
    v = kv[..., QK_WIDTH:].reshape(B, S, N_HEADS_2, V_DIM).transpose(0, 2, 1, 3)
    return k, v

def diff_attention(h, k, v, w_q, lam_vecs, subln, w_o, lambda_init):
    B, S, _ = h.shape
    n_blk = S // Q_BLOCK
    q = (h @ w_q).reshape(B, S, N_HEADS_2, 2, HEAD_DIM_2)
    q = q.reshape(B, n_blk, Q_BLOCK, N_HEADS_2, 2, HEAD_DIM_2).transpose(1, 0, 3, 4, 2, 5)
    lf = lam_vecs.astype(jnp.float32)
    lam = jnp.exp(jnp.sum(lf[0] * lf[1])) - jnp.exp(jnp.sum(lf[2] * lf[3])) + lambda_init
    slopes = jnp.asarray(_alibi_slopes(N_HEADS_2))
    scale = HEAD_DIM_2 ** -0.5
    kf = k.astype(jnp.float32)
    vf = v.astype(jnp.float32)
    key_pos = jnp.arange(S, dtype=jnp.int32)

    def block(args):
        qb, bi = args
        q_pos = bi * Q_BLOCK + jnp.arange(Q_BLOCK, dtype=jnp.int32)
        dist = (q_pos[:, None] - key_pos[None, :]).astype(jnp.float32)
        bias = -slopes[:, None, None] * dist[None]
        s = jnp.einsum('bhitd,bhisd->bhits', qb.astype(jnp.float32), kf) * scale
        s = s + bias[None, :, None]
        s = jnp.where((dist >= 0)[None, None, None], s, -jnp.inf)
        p = jax.nn.softmax(s, axis=-1)
        a = p[:, :, 0] - lam * p[:, :, 1]
        return jnp.einsum('bhts,bhsd->bhtd', a, vf)

    o = lax.map(block, (q, jnp.arange(n_blk, dtype=jnp.int32)))
    o = o.transpose(1, 0, 3, 2, 4).reshape(B, S, N_HEADS_2, V_DIM).astype(h.dtype)
    o = rms_norm_2(o, subln) * (1.0 - lambda_init)
    return o.reshape(B, S, V_WIDTH) @ w_o

def second_inputs(seed: int = 0) -> dict:
    key = jax.random.key(seed)
    ks = jax.random.split(key, 20)
    f32 = jnp.float32

    def w(k, shape, fan_in):
        return jax.random.normal(k, shape, f32) * (fan_in ** -0.5)

    def gain(k, shape):
        return 1.0 + 0.05 * jax.random.normal(k, shape, f32)

    return {
        "x": jax.random.normal(ks[0], (BATCH, SEQ, D_MODEL), f32),
        "a_norm": gain(ks[1], (N_A, D_MODEL)),
        "a_w_in": w(ks[2], (N_A, D_MODEL, 2 * D_GATE), D_MODEL),
        "a_v_norm": gain(ks[3], (N_A, D_GATE)),
        "a_w_sp": w(ks[4], (N_A, N_GROUPS, CHUNK_2, CHUNK_2), CHUNK_2),
        "a_b_sp": 1.0 + 0.1 * jax.random.normal(ks[5], (N_A, N_GROUPS, CHUNK_2), f32),
        "a_w_out": w(ks[6], (N_A, D_GATE, D_MODEL), D_GATE),
        "ffn_norm": gain(ks[7], (DEPTH_2, D_MODEL)),
        "ffn_w_gu": w(ks[8], (DEPTH_2, D_MODEL, 2 * D_FF), D_MODEL),
        "ffn_w_down": w(ks[9], (DEPTH_2, D_FF, D_MODEL), D_FF),
        "kv_norm": gain(ks[10], (D_MODEL,)),
        "kv_w": w(ks[11], (D_MODEL, QK_WIDTH + V_WIDTH), D_MODEL),
        "b_norm": gain(ks[12], (N_B, D_MODEL)),
        "b_w_q": w(ks[13], (N_B, D_MODEL, QK_WIDTH), D_MODEL),
        "b_lambda": 0.1 * jax.random.normal(ks[14], (N_B, 4, HEAD_DIM_2), f32),
        "b_subln": gain(ks[15], (N_B, V_DIM)),
        "b_w_o": w(ks[16], (N_B, V_WIDTH, D_MODEL), V_WIDTH),
        "final_norm": gain(ks[17], (D_MODEL,)),
    }

def second_block(x, a_norm, a_w_in, a_v_norm, a_w_sp, a_b_sp, a_w_out, ffn_norm, ffn_w_gu, ffn_w_down,
              kv_norm, kv_w, b_norm, b_w_q, b_lambda, b_subln, b_w_o, final_norm):
    k = v = None
    for l in range(DEPTH_2):
        if l < N_A:
            x = x + gmlp_mixer(rms_norm_2(x, a_norm[l]), a_w_in[l], a_v_norm[l],
                               a_w_sp[l], a_b_sp[l], a_w_out[l])
        else:
            j = l - N_A
            if j == 0:
                k, v = shared_kv(x, kv_norm, kv_w)
            x = x + diff_attention(rms_norm_2(x, b_norm[j]), k, v, b_w_q[j], b_lambda[j],
                                   b_subln[j], b_w_o[j], _lambda_init(l))
        x = x + swiglu(rms_norm_2(x, ffn_norm[l]), ffn_w_gu[l], ffn_w_down[l])
    return rms_norm_2(x, final_norm)


def setup_inputs(seed=0):
    out = dict(first_inputs(seed))
    for name, value in second_inputs(seed + 1).items():
        if name != "x":
            out[name + "_2"] = value
    return out


def reference(
    x, c, ada_w, ada_b, norm1_g, w_in, conv_w, conv_b, w_q, w_k, b_igate, b_fgate, mlstm_norm_g,
    mlstm_skip, w_pool, b_pool, pool_scale, w_out, norm2_g, w_router_group, b_router_group,
    w_router_expert, b_router_expert, w_expert_gate, w_expert_up, w_expert_down, final_g,
    a_norm_2, a_w_in_2, a_v_norm_2, a_w_sp_2, a_b_sp_2, a_w_out_2, ffn_norm_2, ffn_w_gu_2,
    ffn_w_down_2, kv_norm_2, kv_w_2, b_norm_2, b_w_q_2, b_lambda_2, b_subln_2, b_w_o_2,
    final_norm_2,
):
    x = first_block(
        x, c, ada_w, ada_b, norm1_g, w_in, conv_w, conv_b, w_q, w_k, b_igate, b_fgate,
        mlstm_norm_g, mlstm_skip, w_pool, b_pool, pool_scale, w_out, norm2_g, w_router_group,
        b_router_group, w_router_expert, b_router_expert, w_expert_gate, w_expert_up,
        w_expert_down, final_g,
    )
    return second_block(
        x, a_norm_2, a_w_in_2, a_v_norm_2, a_w_sp_2, a_b_sp_2, a_w_out_2, ffn_norm_2,
        ffn_w_gu_2, ffn_w_down_2, kv_norm_2, kv_w_2, b_norm_2, b_w_q_2, b_lambda_2, b_subln_2,
        b_w_o_2, final_norm_2,
    )


_drawn_inputs = setup_inputs


def setup_inputs(seed=0):
    import zlib

    import numpy as np

    out = dict(_drawn_inputs(seed))
    spreads = {}
    factors = {'b_igate': 200.0,
     'b_router_group': 3.08,
     'b_router_expert': 2.745,
     'b_norm_2': 3.422,
     'b_lambda_2': 5.873,
     'b_subln_2': 3.441}
    for name, (base, spread) in spreads.items():
        noise = np.random.default_rng([zlib.crc32(name.encode()), seed]).standard_normal(out[name].shape)
        drawn = base * np.exp(spread * noise) if base else spread * noise
        out[name] = jnp.asarray(drawn.astype(out[name].dtype))
    for name, factor in factors.items():
        out[name] = (out[name] * factor).astype(out[name].dtype)
    return out
```

```python
from collections import deque
from contextlib import ExitStack
import math

import concourse.bass as bass
from concourse import mybir

F32 = mybir.dt.float32
F32R = mybir.dt.float32r
I32 = mybir.dt.int32
ALU = mybir.AluOpType
ACT = mybir.ActivationFunctionType
AX = mybir.AxisListType.X

P = 128
D = 1024
T = 512
TB = 4
KC = 8
NE = 32
DE = 512
CAP = 128
NOVF = 7
NBLK = NE + NOVF
DFF = 2816
FB = DFF // P
EPS = 1e-6
BIG = 1e30
SLOT = 2048
LAMBDA_INIT = 0.8 - 0.6 * math.exp(-0.3)


class Tok:

    def __init__(self, sem, val=None):
        self.sem, self.val, self.used = sem, val, val is not None


def flat(xs):
    for x in xs:
        if x is None:
            continue
        if isinstance(x, (list, tuple)):
            yield from flat(x)
        else:
            yield x


class Queues:

    def __init__(self, nc, ctx):
        self.nc, self.ctx = nc, ctx
        self.q = {n: [] for n in ("sync", "tensor", "vector", "scalar", "gpsimd")}
        self.sems = {}
        self.part = "main"
        self.last = {}
        self.experts = {}

    def sem(self, name):
        if name not in self.sems:
            self.sems[name] = [self.ctx.enter_context(self.nc.semaphore(name)), 0]
        return self.sems[name]

    def op(self, eng, fn, *after):
        t = Tok(self.sem(f"{self.part}_{eng}"))
        w = list(flat(after))
        for x in w:
            x.used = True
        self.q[eng].append(("op", fn, w, t))
        self.last[eng] = t
        return t

    def dma(self, eng, name, out, in_, *after):
        s = self.sem(name)
        s[1] += 16
        t = Tok(s, s[1])
        w = list(flat(after))
        for x in w:
            x.used = True
        self.q[eng].append(("dma", lambda e: e.dma_start(out, in_), w, t))
        return t

    def gather(self, name, out, out_idx, in_, in_idx, *after):
        s = self.sem(name)
        s[1] += 16
        t = Tok(s, s[1])
        w = list(flat(after))
        for x in w:
            x.used = True
        oo = bass.IndirectOffsetOnAxis(ap=out_idx, axis=0) if out_idx is not None else None
        io = bass.IndirectOffsetOnAxis(ap=in_idx, axis=0) if in_idx is not None else None
        self.q["gpsimd"].append(("dma", lambda e: e.indirect_dma_start(out=out, out_offset=oo, in_=in_, in_offset=io), w, t))
        return t

    def dma_from(self, name, out, n, src, *after):
        s = self.sem(name)
        s[1] += 16
        t = Tok(s, s[1])
        w = list(flat(after))
        for x in w:
            x.used = True
        self.q["sync"].append(("dma", lambda e: e.dma_start(out, src(self.expert(e, n))), w, t))
        return t

    def expert(self, e, n):
        if n not in self.experts:
            r = e.alloc_register(f"expert{n}")
            e.reg_load(r, self.table[0:1, n:n + 1])
            self.experts[n] = e.snap(r, min_val=0, max_val=NE - 1)
        return self.experts[n]

    def wait(self, eng, *after):
        w = list(flat(after))
        for x in w:
            x.used = True
        self.q[eng].append(("wait", None, w, None))

    def enter(self, reg_ap, bound, *after):
        for e in self.q:
            self.wait(e, *after)
            self.q[e].append(("enter", (reg_ap, bound), [], None))

    def leave(self):
        for e in self.q:
            self.q[e].append(("leave", None, [], None))

    def fence(self):
        toks = [t for e, t in self.last.items() if e != "sync"]
        for e in ("tensor", "vector", "scalar", "gpsimd"):
            self.wait(e, toks)
        return toks

    def number(self):
        for items in self.q.values():
            for kind, _, _, t in items:
                if kind == "op" and t.used:
                    t.sem[1] += 1
                    t.val = t.sem[1]

    def run(self, name, eng):
        seen, saved, guards = {}, [], []
        for kind, fn, waits, t in self.q[name]:
            need = {}
            for w in waits:
                if need.get(id(w.sem), (0,))[0] < w.val:
                    need[id(w.sem)] = (w.val, w.sem[0])
            for k, (v, s) in need.items():
                if seen.get(k, 0) < v:
                    seen[k] = v
                    eng.wait_ge(s, v)
            if kind == "op":
                i = fn(eng)
                if t.used:
                    i.then_inc(t.sem[0], 1)
            elif kind == "dma":
                fn(eng).then_inc(t.sem[0], 16)
            elif kind == "enter":
                saved.append(dict(seen))
                r = eng.alloc_register(f"r_{name}_{len(self.q[name])}_{fn[1]}")
                eng.reg_load(r, fn[0])
                g = eng.If_lt(r, fn[1])
                g.__enter__()
                guards.append(g)
            elif kind == "leave":
                guards.pop().__exit__(None, None, None)
                seen = saved.pop()


def program(nc, g, out):
    ctx = ExitStack()
    with ctx:
        K = Queues(nc, ctx)
        scope = [ctx]
        cnt = [0]

        def sb(shape, dt=F32):
            cnt[0] += 1
            return scope[-1].enter_context(nc.sbuf_tensor(f"t{cnt[0]}", shape, dt))

        def push():
            s = ExitStack()
            scope.append(s)

        def pop():
            scope.pop().close()
            return K.fence()

        def V(fn, *a):
            return K.op("vector", fn, *a)

        def A(fn, *a):
            return K.op("scalar", fn, *a)

        def G(fn, *a):
            return K.op("gpsimd", fn, *a)

        def PE(fn, *a):
            return K.op("tensor", fn, *a)

        def act(out_, in_, func, *a, **kw):
            return A(lambda e: e.activation(out_, in_, func, **kw), *a)

        def tt(out_, x, y, op, *a):
            return V(lambda e: e.tensor_tensor(out_, x, y, op), *a)

        def gtt(out_, x, y, op, *a):
            return G(lambda e: e.tensor_tensor(out_, x, y, op), *a)

        def ts(out_, x, s1, s2, o1, o2, *a):
            if o2 is None:
                return V(lambda e: e.tensor_scalar(out_, x, s1, None, o1), *a)
            return V(lambda e: e.tensor_scalar(out_, x, s1, s2, o1, o2), *a)

        def stt(out_, x, s, y, o1, o2, *a):
            return V(lambda e: e.scalar_tensor_tensor(out=out_, in0=x, scalar=s, in1=y, op0=o1, op1=o2), *a)

        def mm(out_, l, r, start, stop, *a):
            return PE(lambda e: e.matmul(out_, l, r, start=start, stop=stop, skip_group_check=True), *a)

        def mm3(out_, l, r, start, stop, *a):
            mm(out_, l[0], r[0], start, False, *a)
            mm(out_, l[0], r[1], False, False)
            return mm(out_, l[1], r[0], False, stop)

        def split(hi, lo, x, *a):
            th = act(hi, x, ACT.Copy, *a)
            tl = tt(lo, x, hi.bitcast(F32), ALU.subtract, th, *a)
            return [th, tl]

        def finish_x(t_x):
            t = K.dma("scalar", "out", out.rearrange("a (t p) d -> p (a t) d", p=P), X[:, :, :], t_x)
            K.wait("scalar", t)
            K.wait("sync", [x[2] for x in loaded])
            while len(scope) > 1:
                scope.pop().close()
            K.number()
            block = ctx.enter_context(nc.Block())

            @block.sync
            def _(eng):
                K.run("sync", eng)

            @block.tensor
            def _(eng):
                K.run("tensor", eng)

            @block.vector
            def _(eng):
                K.run("vector", eng)

            @block.scalar
            def _(eng):
                K.run("scalar", eng)

            @block.gpsimd
            def _(eng):
                K.run("gpsimd", eng)

        banks = [ctx.enter_context(nc.psum_tensor(f"ps{i}", [P, 512], F32)) for i in range(8)]
        bfree = [[] for _ in range(8)]
        bturn = [0]

        def bank():
            b = bturn[0] % 8
            bturn[0] += 1
            return b

        X = sb([P, TB, D])
        XN = sb([P, TB, D])
        ident = sb([P, P])
        onesf = sb([P, P])
        onesr = sb([P, P], F32R)
        epst = sb([P, 1])
        VT = sb([P, P])
        tmpT = [sb([P, 512]) for _ in range(2)]
        small = sb([P, 64])

        t0 = G(lambda e: e.memset(ident[:, :], 0.0))
        t_id = G(lambda e: e.affine_select(out=ident[:, :], in_=ident[:, :], compare_op=ALU.not_equal, fill=1.0,
                                           base=0, pattern=[[-1, P]], channel_multiplier=1), t0)
        t_on = V(lambda e: e.memset(onesf[:, :], 1.0))
        t_one = tt(onesr[:, :], onesf[:, :], onesf[:, :], ALU.mult, t_on)
        t_eps = V(lambda e: e.memset(epst[:, :], EPS))
        xn_d = nc.dram_tensor("xn_d", [T, D], F32, kind="Internal").ap()
        y_d = nc.dram_tensor("y_d", [NBLK * CAP, D], F32, kind="Internal").ap()
        st_d = nc.dram_tensor("st_d", [NBLK * CAP, 1], F32, kind="Internal").ap()
        t_zy = V(lambda e: e.memset(tmpT[0][:, :], 0.0))
        for n in range(NE, NBLK):
            t_yz = K.dma("gpsimd", "yz", y_d[n * CAP:(n + 1) * CAP, :].rearrange("p (a c) -> p a c", a=2),
                         tmpT[0][:, :].unsqueeze(1).broadcast_to([P, 2, 512]), t_zy)

        raws, splits = deque(), deque()

        def add_raw(n, *free):
            for _ in range(n):
                i = len(add_raw.all)
                add_raw.all.append(i)
                raws.append((sb([P, SLOT]), f"raw{i}", list(flat(free))))
        add_raw.all = []

        def add_split(n, *free):
            for _ in range(n):
                splits.append((sb([P, SLOT], F32R), sb([P, SLOT], F32R), list(flat(free))))

        items = []

        def t_item(w, n0):
            items.append(("w", w.rearrange("(c p) n -> p c n", p=P)[:, :, n0:n0 + 256], 8, 256))

        def n_item(w, k0, kn, n0, nn=512):
            items.append(("w", w.rearrange("(c p) n -> p c n", p=P)[:, k0:k0 + kn, n0:n0 + nn], kn, nn))

        ada = g["ada_w"][0].rearrange("(c p) n -> p c n", p=P)

        def ada_items(j):
            for c in range(4):
                items.append(("ada", ada[:, 2 * c:2 * c + 2, j * D:(j + 1) * D], (j, c), None))

        w_in = g["w_in"][0]
        ada_items(0)
        ada_items(1)
        for n0 in (0, 256):
            t_item(w_in, n0)
        for c0 in (1544, 1544 + 256):
            t_item(w_in, c0)
        n_item(w_in, 0, 4, 512)
        n_item(w_in, 4, 4, 512)
        for n0 in (1024, 1280):
            t_item(w_in, n0)
        for j in (2, 3, 4, 5):
            ada_items(j)
        for h in (0, 512):
            for k in (0, 4):
                n_item(g["w_out"][0], k, 4, h)
        for e in range(NE):
            for w in ("w_expert_gate", "w_expert_up"):
                for k in (0, 4):
                    n_item(g[w][0, e], k, 4, 0)
            for k in (0, 2):
                n_item(g["w_expert_down"][0, e], k, 2, 0, 1024)
        for n0 in range(0, 1024, 256):
            t_item(g["a_w_in_2"][0], n0)
        for h in (0, 512):
            for k in (0, 4):
                n_item(g["a_w_in_2"][0], k, 4, 1024 + h)
        for h in (0, 512):
            for k in (0, 4):
                n_item(g["a_w_out_2"][0], k, 4, h)
        FG = [(0, 8), (8, 8), (16, 6)]

        def ffn_items(l):
            for f0, fn in FG:
                for f in range(f0, f0 + fn, 2):
                    t_item(g["ffn_w_gu_2"][l], f * P)
                    t_item(g["ffn_w_gu_2"][l], DFF + f * P)
                for h in (0, 512):
                    for k in range(0, fn, 4):
                        n_item(g["ffn_w_down_2"][l], f0 + k, min(4, fn - k), h)

        ffn_items(0)
        for n0 in range(0, 1024, 256):
            t_item(g["b_w_q_2"][0], n0)
        for h in (0, 512):
            for k in (0, 4):
                n_item(g["kv_w_2"], k, 4, 1024 + h)
        for n0 in range(0, 1024, 256):
            t_item(g["kv_w_2"], n0)
        for h in (0, 512):
            for k in (0, 4):
                n_item(g["b_w_o_2"][0], k, 4, h)
        ffn_items(1)

        loaded = deque()
        ready = deque()
        nl = [0]
        npz = [0]

        def load_more():
            while raws and nl[0] < len(items):
                kind, ap, a_, b_ = items[nl[0]]
                ten, name, free = raws.popleft()
                n = ap.shape[1] * ap.shape[2]
                dst = ten[:, 0:n].rearrange("p (c n) -> p c n", c=ap.shape[1])
                t = K.dma("sync", name, dst, ap, free)
                loaded.append((ten, name, t))
                nl[0] += 1

        def prep_one(forced):
            if npz[0] >= len(items):
                return False
            kind, ap, a_, b_ = items[npz[0]]
            if kind == "ada" and not forced:
                return False
            if kind == "w" and not splits:
                return False
            load_more()
            ten, name, t = loaded.popleft()
            npz[0] += 1
            if kind == "ada":
                tl = ada_step(a_[0], a_[1], ten, t)
                raws.append((ten, name, [tl]))
            else:
                n = a_ * b_
                hi, lo, free = splits.popleft()
                th = act(hi[:, 0:n], ten[:, 0:n], ACT.Copy, t, free)
                tl = tt(lo[:, 0:n], ten[:, 0:n], hi[:, 0:n].bitcast(F32), ALU.subtract, th, free)
                raws.append((ten, name, [th, tl]))
                v = lambda z: z[:, 0:n].rearrange("p (c n) -> p c n", c=a_)
                ready.append((v(hi), v(lo), [th, tl], hi, lo))
            load_more()
            return True

        def take():
            while not ready:
                assert prep_one(True)
            while prep_one(False):
                pass
            return ready.popleft()

        def done(w, *toks):
            splits.append((w[3], w[4], list(flat(toks))))

        def pump(n):
            for _ in range(n):
                if npz[0] < len(items) and items[npz[0]][0] == "ada":
                    prep_one(True)

        GF = sb([P, D])
        RB = sb([P, 36])
        SLK = sb([P, 2, TB], I32)
        CT = sb([1, 8], I32)
        K.table = CT
        TOK = sb([P, NBLK], I32)
        add_raw(3)
        add_split(2)
        push()
        tri = sb([P, P])
        neg = sb([P, P])
        sel = sb([4, 4 * P])
        VR = sb([P, P])
        BR = sb([48, P])
        BT = sb([P, 48])
        t0 = G(lambda e: e.memset(neg[:, :], 0.0))
        t_neg = G(lambda e: e.affine_select(out=neg[:, :], in_=neg[:, :], compare_op=ALU.is_ge, fill=-BIG,
                                            base=0, pattern=[[1, P]], channel_multiplier=-1), t0)
        t0 = G(lambda e: e.memset(sel[:, :], 0.0))
        sv = sel[:, :].rearrange("k (h p) -> k h p", h=4)
        t_sel = G(lambda e: e.affine_select(out=sv, in_=sv, compare_op=ALU.not_equal, fill=1.0,
                                            base=0, pattern=[[1, 4], [0, P]], channel_multiplier=-1), t0)
        t0 = G(lambda e: e.memset(tri[:, :], 1.0))
        t_tri = G(lambda e: e.affine_select(out=tri[:, :], in_=tri[:, :], compare_op=ALU.is_gt, fill=0.0,
                                            base=0, pattern=[[1, P]], channel_multiplier=-1), t0)

        vec = {}
        row = 0
        t_vr = []
        for name, ap, n in (
            ("c", g["c"], 8), ("n1", g["norm1_g"], 8), ("an", g["a_norm_2"], 8), ("fn", g["ffn_norm_2"], 16),
            ("kvn", g["kv_norm_2"], 8), ("bn", g["b_norm_2"], 8), ("cw", g["conv_w"], 16), ("cb", g["conv_b"], 4),
            ("mn", g["mlstm_norm_g"], 4), ("sk", g["mlstm_skip"], 4), ("bp", g["b_pool"], 4),
            ("psc", g["pool_scale"], 4), ("av", g["a_v_norm_2"], 8), ("sub", g["b_subln_2"], 1),
        ):
            ap = ap.rearrange({1: "(r p) -> r p", 2: "a (r p) -> (a r) p", 3: "a b (r p) -> (a b r) p"}[len(ap.shape)], p=P)
            t_vr.append(K.dma("scalar", "vr", VR[row:row + n, :], ap))
            vec[name] = row
            row += n
        NV = row
        t_x = [K.dma("scalar", "x", X[:, :, :], g["x"].rearrange("a (t p) d -> p (a t) d", p=P))]
        t_br = K.dma("scalar", "br", BR[:, :], g["ada_b"].rearrange("a (r p) -> (a r) p", p=P))
        b = bank()
        t0 = PE(lambda e, b=b: e.transpose(banks[b][:, 0:NV], VR[0:NV, :], ident[0:NV, 0:NV]), t_vr, t_id)
        t0b = PE(lambda e, b=b: e.transpose(banks[b][:, 128:176], BR[:, :], ident[0:48, 0:48]), t_br)
        t_vt = V(lambda e, b=b: e.tensor_copy(VT[:, 0:NV], banks[b][:, 0:NV]), t0, t0b)
        t_bt = V(lambda e, b=b: e.tensor_copy(BT[:, :], banks[b][:, 128:176]), t0b)
        bfree[b] = [t_vt, t_bt]

        def col(name, i):
            return VT[:, vec[name] + i:vec[name] + i + 1]

        GA, G2, S2 = sb([P, D]), sb([P, D]), sb([P, D])
        acc = [sb([P, D]) for _ in range(2)]
        acc_t = [None, None]
        sc = sb([P, 8])
        modc = sb([P, 16])
        t_sc = act(sc[:, :], VT[:, vec["c"]:vec["c"] + 8], ACT.Silu, t_vt)
        t_gb = K.dma("scalar", "g2", G2[:, :], g["norm2_g"].partition_broadcast(P).rearrange("p a d -> p (a d)"))
        t_g1 = [None]
        t_mod = {}

        def ada_step(j, c, ten, t):
            ac = acc[j % 2]
            if c == 0:
                t0 = G(lambda e: e.memset(ac[:, :], 0.0), acc_t[j % 2])
                acc_t[j % 2] = K.dma("scalar", f"adab{j % 2}", ac[0:1, :], g["ada_b"][:, j * D:(j + 1) * D], t0)
            tp = acc_t[j % 2]
            for i in range(2):
                tp = stt(ac[:, :], ten[:, i * D:(i + 1) * D], sc[:, 2 * c + i:2 * c + i + 1], ac[:, :],
                         ALU.mult, ALU.add, tp, t, t_sc)
            acc_t[j % 2] = tp
            if c == 3:
                acc_t[j % 2] = ada_end(j, ac, tp)
            return tp

        def ada_end(j, ac, tp):
            if j < 2:
                b = bank()
                for k in range(KC):
                    tm = mm(banks[b][:, k:k + 1], ac[:, k * P:(k + 1) * P], onesf[:, 0:1], True, True,
                            tp, t_on, bfree[b] if k == 0 else None)
                if j == 0:
                    t = V(lambda e: e.tensor_copy(modc[:, 0:8], banks[b][:, 0:8]), tm)
                else:
                    t = stt(modc[:, 8:16], banks[b][:, 0:8], 1.0, VT[:, vec["n1"]:vec["n1"] + 8],
                            ALU.add, ALU.mult, tm, t_vt)
                bfree[b] = [t]
                t_mod[j] = t
                return tm
            for h in range(2):
                b = bank()
                hs = slice(h * 512, (h + 1) * 512)
                tm = mm(banks[b][:, :], onesf[:, :], ac[:, hs], True, True, tp, t_on, bfree[b])
                if j == 4:
                    t = stt(G2[:, hs], banks[b][:, :], 1.0, G2[:, hs], ALU.add, ALU.mult, tm, t_gb)
                else:
                    dst = {2: GA, 3: S2, 5: GF}[j]
                    t = act(dst[:, hs], banks[b][:, :], ACT.Copy, tm)
                bfree[b] = [t]
                t_mod.setdefault(j, []).append(t)
            return tm

        def rstd_of(t_in, n=D):
            tq = []
            for tb in range(TB):
                tq.append(act(XN[:, tb, :], X[:, tb, :], ACT.Square, t_in, accum_out=small[:, tb:tb + 1]))
            t0 = act(small[:, 4:8], small[:, 0:4], ACT.Sqrt, tq, t_eps, scale=1.0 / D, bias=epst[:, 0:1])
            return V(lambda e: e.reciprocal(small[:, 8:12], small[:, 4:8]), t0)

        def normalize(t_in):
            tr = rstd_of(t_in)
            return [ts(XN[:, tb, :], X[:, tb, :], small[:, 8 + tb:9 + tb], None, ALU.mult, None, tr)
                    for tb in range(TB)]

        tmp_free = [[t_yz], []]
        tmp_turn = [0]

        def to_features(hT, t_xn, gcols, scols, *t_cols):
            toks, pend = [], []

            def finish(kc, tt_, i):
                th = act(hT[0][:, kc, :], tmpT[i][:, :], ACT.Copy, tt_)
                tl = tt(hT[1][:, kc, :], tmpT[i][:, :], hT[0][:, kc, :].bitcast(F32), ALU.subtract, th)
                tmp_free[i] = [th, tl]
                toks.extend([th, tl])

            for kc in range(KC):
                b = bank()
                for tb in range(TB):
                    tm = PE(lambda e, b=b, tb=tb, kc=kc: e.transpose(banks[b][:, tb * P:(tb + 1) * P],
                                                                    XN[:, tb, kc * P:(kc + 1) * P], ident[:, :]),
                            t_xn, t_id, bfree[b])
                i = tmp_turn[0] % 2
                tmp_turn[0] += 1
                if gcols is None:
                    t = V(lambda e, b=b, i=i: e.tensor_copy(tmpT[i][:, :], banks[b][:, :]), tm, tmp_free[i])
                elif scols is None:
                    t = ts(tmpT[i][:, :], banks[b][:, :], gcols(kc), None, ALU.mult, None, tm, tmp_free[i], t_cols)
                else:
                    t = ts(tmpT[i][:, :], banks[b][:, :], gcols(kc), scols(kc), ALU.mult, ALU.add, tm,
                           tmp_free[i], t_cols)
                bfree[b] = [t]
                if pend:
                    finish(*pend.pop())
                pend.append((kc, t, i))
            finish(*pend.pop())
            return toks

        def t_blocks(hT, t_h, n):
            for _ in range(n):
                w = take()
                for j in range(2):
                    b = bank()
                    for kc in range(KC):
                        tm = mm3(banks[b][:, :], [w[i][:, kc, j * P:(j + 1) * P] for i in (0, 1)],
                                 [hT[i][:, kc, :] for i in (0, 1)], kc == 0, kc == KC - 1, w[2], t_h,
                                 bfree[b] if kc == 0 else None)
                    if j == 1:
                        done(w, tm)
                    yield b, tm

        def n_blocks(hT, t_h, nk):
            bs = [bank() for _ in range(TB)]
            tms = [None] * TB
            k0 = 0
            while k0 < nk:
                w = take()
                kn = w[0].shape[1]
                for tb in range(TB):
                    for k in range(kn):
                        tms[tb] = mm3(banks[bs[tb]][:, :], [hT[i][:, k0 + k, tb * P:(tb + 1) * P] for i in (0, 1)],
                                      [w[i][:, k, :] for i in (0, 1)], k0 + k == 0, k0 + k == nk - 1, w[2], t_h,
                                      bfree[bs[tb]] if k0 + k == 0 else None)
                done(w, tms[TB - 1])
                k0 += kn
            return list(zip(bs, tms))

        def add_to_x(hT, t_h, nk, gate=None, t_gate=None):
            toks = []
            for h in range(2):
                hs = slice(h * 512, (h + 1) * 512)
                for tb, (b, tm) in enumerate(n_blocks(hT, t_h, nk)):
                    if gate is None:
                        t = tt(X[:, tb, hs], X[:, tb, hs], banks[b][:, :], ALU.add, tm)
                        bfree[b] = [t]
                    else:
                        i = tmp_turn[0] % 2
                        tmp_turn[0] += 1
                        t = tt(tmpT[i][:, :], banks[b][:, :], gate[:, hs], ALU.mult, tm, t_gate, tmp_free[i])
                        bfree[b] = [t]
                        t = tt(X[:, tb, hs], X[:, tb, hs], tmpT[i][:, :], ALU.add, t)
                        tmp_free[i] = [t]
                    toks.append(t)
            return toks

        hTh = [sb([P, KC, T], F32R), sb([P, KC, T], F32R)]
        t_xn = normalize(t_x)
        pump(8)
        t_h = to_features(hTh, t_xn, lambda kc: modc[:, 8 + kc:9 + kc], lambda kc: modc[:, kc:kc + 1],
                          t_mod[0], t_mod[1])
        UC = [XN[:, 0, 0:512], XN[:, 0, 512:1024], XN[:, 1, 0:512], XN[:, 1, 512:1024]]
        SO = [XN[:, 2, 0:512], XN[:, 2, 512:1024], XN[:, 3, 0:512], XN[:, 3, 512:1024]]
        VN = sb([P, TB, 512])
        AR = [sb([P, 1024], F32R) for _ in range(2)]
        RM = sb([4, 2, 512])
        UP = [sb([P, 515]) for _ in range(2)]
        CY = [sb([P, 512]) for _ in range(2)]
        WQ = sb([P, 3, 4, P])
        W2 = [[sb([P, P], F32R), sb([P, P], F32R)] for _ in range(2)]
        EM, HH = sb([P, T]), sb([P, T])
        push()
        PT = sb([P, 4, 528])
        WIF = sb([P, KC, 8])
        WIh = [a[:, :].rearrange("p (c n) -> p c n", c=KC) for a in AR]
        t_wif = K.dma("scalar", "wif", WIF[:, :, :], w_in.rearrange("(c p) n -> p c n", p=P)[:, :, 1536:1544])
        tz = [V(lambda e, z=z: e.memset(z[:, :].bitcast(F32), 0.0)) for z in AR]
        t_wi = []
        for j in range(2):
            s = WIh[0][:, :, 32 * j:32 * j + 4]
            th = act(s, WIF[:, :, 4 * j:4 * j + 4], ACT.Copy, t_wif, tz)
            tl = tt(WIh[1][:, :, 32 * j:32 * j + 4], WIF[:, :, 4 * j:4 * j + 4], s.bitcast(F32), ALU.subtract,
                    th, tz, t_wif)
            t_wi += [th, tl]
        BIF = sb([4, 2])
        t_bif = [K.dma("scalar", "bif", BIF[:, 0:1], g["b_igate"].rearrange("a h -> h a")),
                 K.dma("scalar", "bif", BIF[:, 1:2], g["b_fgate"].rearrange("a h -> h a"))]
        b = bank()
        for kc in range(KC):
            tm = mm3(banks[b][:, :], [WIh[i][:, kc, :] for i in (0, 1)], [hTh[i][:, kc, :] for i in (0, 1)],
                     kc == 0, kc == KC - 1, t_wi, t_h, bfree[b] if kc == 0 else None)
        t_if = tm
        R = [PT[0:4, j, 0:512] for j in range(4)]
        t_i = ts(R[0], banks[b][0:4, :], BIF[:, 0:1], None, ALU.add, None, tm, t_bif)
        t_f = ts(R[1], banks[b][32:36, :], BIF[:, 1:2], None, ALU.add, None, tm, t_bif)
        bfree[b] = [t_i, t_f]
        t = act(R[2], R[1], ACT.Abs, t_f)
        t = act(R[2], R[2], ACT.Exp, t, scale=-1.0)
        t = act(R[2], R[2], ACT.Ln, t, t_on, bias=onesf[0:4, 0:1])
        t = stt(R[1], R[1], 0.0, R[2], ALU.min, ALU.subtract, t)
        tz = V(lambda e: e.memset(R[2], 0.0), t)
        t_b = V(lambda e: e.tensor_tensor_scan(R[3], R[1], R[2], 0.0, ALU.add, ALU.add), t, tz)
        t_r = tt(R[0], R[0], R[3], ALU.subtract, t_b, t_i)
        t = V(lambda e: e.tensor_tensor_scan(R[2], R[0], R[0], 0.0, ALU.max, ALU.max), t_r)
        t_nM = ts(RM[:, 0, :], R[2], -1.0, None, ALU.mult, None, t)
        t_nm = stt(RM[:, 1, :], R[3], -1.0, R[2], ALU.mult, ALU.subtract, t)
        b = bank()
        for tb in range(TB):
            tm = PE(lambda e, b=b, tb=tb: e.transpose(banks[b][:, 4 * tb:4 * tb + 4], R[0][:, tb * P:(tb + 1) * P],
                                                     ident[0:4, 0:4]), t_r, bfree[b])
        rcol = small[:, 16:32]
        t_rc = V(lambda e, b=b: e.tensor_copy(rcol, banks[b][:, 0:16]), tm)
        bfree[b] = [t_rc]

        up_free = [None, None]
        cy_free = [None, None]
        t_up0 = [V(lambda e, z=z: e.memset(z[:, 0:3], 0.0)) for z in UP]
        t_uc = []
        for cb, (b, tm) in enumerate(t_blocks(hTh, t_h, 2)):
            i = cb % 2
            t = V(lambda e, b=b, i=i: e.tensor_copy(UP[i][:, 3:515], banks[b][:, :]), tm, up_free[i])
            bfree[b] = [t]
            t = ts(CY[i][:, :], UP[i][:, 0:512], col("cw", cb), col("cb", cb), ALU.mult, ALU.add, t, t_up0,
                   t_vt, cy_free[i])
            for k in range(1, 4):
                t = stt(CY[i][:, :], UP[i][:, k:k + 512], col("cw", 4 * k + cb), CY[i][:, :], ALU.mult, ALU.add, t)
            up_free[i] = t
            t = act(UC[cb], CY[i][:, :], ACT.Silu, t, t_h)
            cy_free[i] = t
            t_uc.append(t)
        t_pz = V(lambda e: e.memset(PT[:, :, 0:16], 0.0), t_rc, t_nM, t_nm)
        t_pt = []
        for gi, (b, tm) in enumerate(t_blocks(hTh, t_h, 2)):
            t = act(PT[:, gi, 16:528], banks[b][:, :], ACT.Copy, tm, t_rc, t_nM, t_nm)
            bfree[b] = [t]
            t_pt.append(t)
        t_v = []
        for tb, (b, tm) in enumerate(n_blocks(hTh, t_h, KC)):
            t = act(VN[:, tb, :], banks[b][:, :], ACT.Copy, tm)
            bfree[b] = [t]
            t_v.append(t)
        t_so = []
        for cb, (b, tm) in enumerate(t_blocks(hTh, t_h, 2)):
            t = act(SO[cb], banks[b][:, :], ACT.Sigmoid, tm)
            bfree[b] = [t]
            t_so.append(t)
        t_hfree = [tm]
        mixT = hTh
        t_wq = [K.dma("scalar", "wq", WQ[:, 0, :, :], g["w_q"][0].rearrange("h d e -> d h e")),
                K.dma("scalar", "wq", WQ[:, 1, :, :], g["w_k"][0].rearrange("h d e -> d h e")),
                K.dma("scalar", "wq", WQ[:, 2, :, :], g["w_pool"][0].rearrange("h d e -> d h e"))]
        RC = sb([P, 16])
        RI = sb([P, 16], I32)
        t0 = G(lambda e: e.iota(RI[:, :], pattern=[[1, 16]], base=1, channel_multiplier=0))
        t0 = V(lambda e: e.tensor_copy(RC[:, :], RI[:, :]), t0)
        t_rcn = V(lambda e: e.reciprocal(RC[:, :], RC[:, :]), t0)
        SW = [[a[:, 0:512], a[:, 512:1024]] for a in AR]
        w2_free = [[], []]
        sw_free = [[t_if], [t_if]]
        mix_toks = []
        PW = [CY[0], CY[1]]
        PA_ = [sb([P, 528]), sb([P, 528])]
        pfree = [cy_free[0], cy_free[1]]
        pa_tok = None
        tmp2_free = [[], []]
        for gi in range(4):
            src, t = PT[:, gi, :], [t_pt[gi], t_pz]
            sh = 1
            for s in range(gi + 1):
                dst = PA_[s % 2]
                lo = 2 * sh - 1
                t = gtt(dst[:, lo:528], src[:, lo:528], src[:, lo - sh:528 - sh], ALU.add, t, pa_tok)
                src = dst
                sh *= 2
            Wn = 2 ** (gi + 1)
            pw = PW[gi % 2]
            t1 = ts(pw[:, :], src[:, 16:528], 1.0 / Wn, None, ALU.mult, None, t, pfree[gi % 2])
            t2 = tt(pw[:, 0:Wn], src[:, 16:16 + Wn], RC[:, 0:Wn], ALU.mult, t, t1, t_rcn)
            pa_tok = t2
            t3 = tt(pw[:, :], pw[:, :], PT[:, gi, 16:528], ALU.subtract, t2)
            tw = split(W2[gi % 2][0][:, :], W2[gi % 2][1][:, :], WQ[:, 2, gi, :], t_wq, w2_free[gi % 2])
            tsx = split(SW[gi % 2][0], SW[gi % 2][1], pw[:, :], t3, sw_free[gi % 2])
            pfree[gi % 2] = tsx
            b = bank()
            tm = mm3(banks[b][:, :], [W2[gi % 2][i][:, :] for i in (0, 1)], [SW[gi % 2][i] for i in (0, 1)],
                     True, True, tw, tsx, bfree[b])
            w2_free[gi % 2] = [tm]
            sw_free[gi % 2] = [tm]
            i = tmp_turn[0] % 2
            tmp_turn[0] += 1
            t = ts(tmpT[i][:, :], banks[b][:, :], col("bp", gi), col("psc", gi), ALU.add, ALU.mult, tm, tmp_free[i])
            bfree[b] = [t]
            tmp_free[i] = split(mixT[0][:, 4 + gi, :], mixT[1][:, 4 + gi, :], tmpT[i][:, :], t, t_hfree)
            mix_toks += tmp_free[i]
        pop()
        push()
        UCs = SW[0]
        Qs = [sb([P, T], F32R), sb([P, T], F32R)]
        Ks = [sb([P, T], F32R), sb([P, T], F32R)]
        Vs = [sb([P, TB, P], F32R), sb([P, TB, P], F32R)]
        ND, DG = CY
        EE = [z[:, 0:T] for z in UP]
        ee_free = [[], []]
        last = []
        for h in range(4):
            pump(4)
            tw = []
            for z in range(2):
                tw += split(W2[z][0][:, :], W2[z][1][:, :], WQ[:, z, h, :], t_wq, w2_free[z])
            tu = split(UCs[0], UCs[1], UC[h], t_uc[h], last, sw_free[0])
            tv = split(Vs[0][:, :, :], Vs[1][:, :, :], VN[:, :, h * P:(h + 1) * P], t_v, last)
            bq, bk = bank(), bank()
            tqm = mm3(banks[bq][:, :], [W2[0][i][:, :] for i in (0, 1)], [UCs[i] for i in (0, 1)],
                      True, True, tw, tu, bfree[bq])
            tkm = mm3(banks[bk][:, :], [W2[1][i][:, :] for i in (0, 1)], [UCs[i] for i in (0, 1)],
                      True, True, tw, tu, bfree[bk])
            w2_free = [[tqm], [tkm]]
            sw_free[0] = [tkm]
            i = tmp_turn[0] % 2
            tmp_turn[0] += 2
            t = ts(tmpT[i][:, :], banks[bq][:, :], float(P) ** -0.5, None, ALU.mult, None, tqm, tmp_free[i])
            bfree[bq] = [t]
            tq = split(Qs[0][:, :], Qs[1][:, :], tmpT[i][:, :], t, last)
            tmp_free[i] = tq
            j = 1 - i
            t = V(lambda e, bk=bk, j=j: e.tensor_copy(tmpT[j][:, :], banks[bk][:, :]), tkm, tmp_free[j])
            bfree[bk] = [t]
            tk = split(Ks[0][:, :], Ks[1][:, :], tmpT[j][:, :], t, last)
            tmp_free[j] = tk
            b = bank()
            tm = mm(banks[b][:, :], sel[:, h * P:(h + 1) * P], RM[:, 0, :], True, True, t_nM, t_sel, bfree[b])
            t_nd = V(lambda e, b=b: e.tensor_copy(ND[:, :], banks[b][:, :]), tm, last)
            bfree[b] = [t_nd]
            t_dg = tt(DG[:, :].rearrange("p (a c) -> p a c", a=4), ND[:, :].rearrange("p (a c) -> p a c", a=4),
                      neg[:, :].unsqueeze(1).broadcast_to([P, 4, P]), ALU.add, t_nd, t_neg, last)
            b = bank()
            tm = mm(banks[b][:, :], sel[:, h * P:(h + 1) * P], RM[:, 1, :], True, True, t_nm, t_sel, bfree[b])
            t_em = act(EM[:, :], banks[b][:, :], ACT.Exp, tm, last)
            bfree[b] = [t_em]
            bn, bd = bank(), bank()
            for s in range(TB):
                z = s % 2
                n = T - s * P
                cs = slice(s * P, T)
                b = bank()
                tm = mm3(banks[b][:, 0:n], [Ks[i][:, s * P:(s + 1) * P] for i in (0, 1)],
                         [Qs[i][:, cs] for i in (0, 1)], True, True, tq, tk, bfree[b])
                rc = small[:, 16 + 4 * s + h:17 + 4 * s + h]
                te = [act(EE[z][:, 0:P], DG[:, s * P:(s + 1) * P], ACT.Exp, t_dg, t_rc, ee_free[z], bias=rc)]
                if n > P:
                    te.append(act(EE[z][:, P:n], ND[:, (s + 1) * P:T], ACT.Exp, t_nd, t_rc, ee_free[z], bias=rc))
                t = tt(EE[z][:, 0:n], EE[z][:, 0:n], banks[b][:, 0:n], ALU.mult, tm, te)
                bfree[b] = [t]
                tsw = split(SW[z][0][:, 0:n], SW[z][1][:, 0:n], EE[z][:, 0:n], t, sw_free[z])
                ee_free[z] = tsw
                tn = mm3(banks[bn][:, cs], [Vs[i][:, s, :] for i in (0, 1)], [SW[z][i][:, 0:n] for i in (0, 1)],
                         s == 0, s == 3, tv, tsw, bfree[bn] if s == 0 else None)
                mm(banks[bd][:, cs], onesr[:, :], SW[z][0][:, 0:n], s == 0, False, t_one,
                   bfree[bd] if s == 0 else None)
                td = mm(banks[bd][:, cs], onesr[:, :], SW[z][1][:, 0:n], False, s == 3)
                sw_free[z] = [td]
            t = act(DG[:, :], banks[bd][:, :], ACT.Abs, td, te)
            bfree[bd] = [t]
            t = tt(EM[:, :], EM[:, :], DG[:, :], ALU.max, t, t_em)
            t = V(lambda e: e.reciprocal(EM[:, :], EM[:, :]), t)
            t_hh = tt(HH[:, :], banks[bn][:, :], EM[:, :], ALU.mult, t, tn, last)
            bfree[bn] = [t_hh]
            t = act(ND[:, :], HH[:, :], ACT.Square, t_hh, te)
            b = bank()
            tm = mm(banks[b][:, :], onesf[:, :], ND[:, :], True, True, t, bfree[b])
            t = act(DG[:, :], banks[b][:, :], ACT.Sqrt, tm, scale=1.0 / P, bias=epst[:, 0:1])
            bfree[b] = [t]
            t = V(lambda e: e.reciprocal(DG[:, :], DG[:, :]), t)
            t = stt(HH[:, :], HH[:, :], col("mn", h), DG[:, :], ALU.mult, ALU.mult, t)
            t = stt(HH[:, :], UC[h], col("sk", h), HH[:, :], ALU.mult, ALU.add, t)
            t = tt(HH[:, :], HH[:, :], SO[h], ALU.mult, t, t_so)
            tf = split(mixT[0][:, h, :], mixT[1][:, h, :], HH[:, :], t, t_hfree)
            mix_toks += tf
            last = [tm, tf, td, tn]
        t_x = add_to_x(mixT, mix_toks, KC, GA, t_mod[2])
        pop()

        t_xn = normalize(t_x)
        toks = []
        for tb in range(TB):
            t = tt(XN[:, tb, :], XN[:, tb, :], G2[:, :], ALU.mult, t_xn, t_mod[4])
            t = tt(XN[:, tb, :], XN[:, tb, :], S2[:, :], ALU.add, t, t_mod[3])
            toks.append(t)
        t_xd = K.dma("scalar", "xnd", xn_d.rearrange("(t p) d -> p t d", p=P), XN[:, :, :], toks)
        t_h = to_features(hTh, toks, None, None)
        push()
        WR = sb([P, KC, 36])
        WRs = [sb([P, KC, 36], F32R), sb([P, KC, 36], F32R)]
        t_wr = [K.dma("scalar", "wr", WR[:, :, 0:4], g["w_router_group"][0].rearrange("(c p) n -> p c n", p=P)),
                K.dma("scalar", "wr", WR[:, :, 4:36], g["w_router_expert"][0].rearrange("(c p) n -> p c n", p=P)),
                K.dma("scalar", "wr", RB[:, 0:4], g["b_router_group"].partition_broadcast(P).rearrange("p a d -> p (a d)")),
                K.dma("scalar", "wr", RB[:, 4:36], g["b_router_expert"].partition_broadcast(P).rearrange("p a d -> p (a d)"))]
        t_ws = split(WRs[0][:, :, :], WRs[1][:, :, :], WR[:, :, :], t_wr)
        b = bank()
        for tb in range(TB):
            for kc in range(KC):
                tm = mm3(banks[b][:, tb * 36:(tb + 1) * 36], [hTh[i][:, kc, tb * P:(tb + 1) * P] for i in (0, 1)],
                         [WRs[i][:, kc, :] for i in (0, 1)], kc == 0, kc == KC - 1, t_h, t_ws, bfree[b])
        LG = sb([P, TB, 36])
        t_lg = tt(LG[:, :, :], banks[b][:, 0:144].rearrange("p (t n) -> p t n", t=TB),
                  RB[:, :].unsqueeze(1).broadcast_to([P, TB, 36]), ALU.add, tm)
        bfree[b] = [t_lg]
        CI = sb([P, 72], I32)
        CJ = sb([P, 72])
        t0 = [G(lambda e: e.iota(CI[:, 0:4], pattern=[[-1, 4]], base=4, channel_multiplier=0)),
              G(lambda e: e.iota(CI[:, 4:36], pattern=[[-1, 32]], base=32, channel_multiplier=0)),
              G(lambda e: e.iota(CI[:, 36:68], pattern=[[1, 32]], base=0, channel_multiplier=0)),
              G(lambda e: e.iota(CI[:, 68:72], pattern=[[P, 4]], base=0, channel_multiplier=1))]
        t_cj = V(lambda e: e.tensor_copy(CJ[:, :], CI[:, :]), t0)
        EJ = CJ[:, 36:68]

        def red(out_, in_, op, *a):
            return V(lambda e: e.tensor_reduce(out_, in_, AX, op), *a)

        def bc(x, n):
            return x.unsqueeze(2).broadcast_to([P, TB, n])

        def bt(x, n):
            return x.unsqueeze(1).broadcast_to([P, TB, n])

        S = sb([P, 24, TB])
        sx = lambda i: S[:, i, :]
        W4 = sb([P, TB, 4])
        OG = sb([P, TB, 4])
        LE = sb([P, TB, 32])
        W32 = sb([P, TB, 32])
        OH = [sb([P, TB, 32]) for _ in range(2)]
        AA = sb([P, TB, 32])
        gl = LG[:, :, 0:4]
        t = red(sx(0), gl, ALU.max, t_lg)
        t1 = tt(W4[:, :, :], gl, bc(sx(0), 4), ALU.is_equal, t)
        t1 = tt(W4[:, :, :], W4[:, :, :], bt(CJ[:, 0:4], 4), ALU.mult, t1, t_cj)
        t1 = red(sx(1), W4[:, :, :], ALU.max, t1)
        t_og = tt(OG[:, :, :], W4[:, :, :], bc(sx(1), 4), ALU.is_equal, t1)
        t1 = tt(W4[:, :, :], gl, bc(sx(0), 4), ALU.subtract, t_og)
        t1 = act(W4[:, :, :], W4[:, :, :], ACT.Exp, t1)
        t1 = red(sx(2), W4[:, :, :], ALU.add, t1)
        t_pg = V(lambda e: e.reciprocal(sx(3), sx(2)), t1)
        t = ts(OG[:, :, :], OG[:, :, :], -1.0, BIG, ALU.add, ALU.mult, t_og)
        t_le = None
        for tb in range(TB):
            t_le = tt(LE[:, tb, :].rearrange("p (a c) -> p a c", a=4), LG[:, tb, 4:36].rearrange("p (a c) -> p a c", a=4),
                      OG[:, tb, :].unsqueeze(2).broadcast_to([P, 4, 8]), ALU.add, t, t_lg)
        tv = []
        t = t_le
        for k in range(2):
            t = red(sx(4 + k), LE[:, :, :], ALU.max, t)
            t = tt(W32[:, :, :], LE[:, :, :], bc(sx(4 + k), 32), ALU.is_equal, t)
            t = tt(W32[:, :, :], W32[:, :, :], bt(CJ[:, 4:36], 32), ALU.mult, t)
            t = red(sx(6), W32[:, :, :], ALU.max, t)
            t = tt(OH[k][:, :, :], W32[:, :, :], bc(sx(6), 32), ALU.is_equal, t)
            if k == 0:
                t = stt(LE[:, :, :], OH[0][:, :, :], -2.0 * BIG, LE[:, :, :], ALU.mult, ALU.add, t)
        t_oh = t
        t = tt(sx(7), sx(5), sx(4), ALU.subtract, t_oh)
        t = act(sx(7), sx(7), ACT.Exp, t)
        t1 = ts(sx(8), sx(7), 1.0, None, ALU.add, None, t)
        t1 = V(lambda e: e.reciprocal(sx(8), sx(8)), t1)
        GT = sb([P, 2, TB])
        t1 = tt(small[:, 32:36], sx(8), sx(3), ALU.mult, t1, t_pg)
        t_gt = tt(small[:, 36:40], small[:, 32:36], sx(7), ALU.mult, t1)
        t_a = tt(AA[:, :, :], OH[0][:, :, :], OH[1][:, :, :], ALU.add, t_oh)
        b = bank()
        for tb in range(TB):
            for s in range(tb + 1):
                tm = mm(banks[b][:, tb * 32:(tb + 1) * 32], tri[:, :] if s == tb else onesf[:, :], AA[:, s, :],
                        s == 0, s == tb, t_a, t_tri, bfree[b])
        for s in range(TB):
            tm = mm(banks[b][:, 128:160], onesf[:, :], AA[:, s, :], s == 0, s == 3)
        RK = sb([P, 160])
        t_rk = V(lambda e, b=b: e.tensor_copy(RK[:, :], banks[b][:, 0:160]), tm)
        bfree[b] = [t_rk]
        CN = RK[:, 128:160]
        NO = sb([P, 5, 32])
        t = ts(NO[:, 0, :], CN, float(CAP), None, ALU.is_gt, None, t_rk)
        t = stt(NO[:, 0, :], CN, 2.0 * CAP, NO[:, 0, :], ALU.is_gt, ALU.add, t)
        t = stt(NO[:, 0, :], CN, 3.0 * CAP, NO[:, 0, :], ALU.is_gt, ALU.add, t)
        tz = V(lambda e: e.memset(NO[:, 4, :], 0.0))
        t_in = V(lambda e: e.tensor_tensor_scan(NO[:, 1, :], NO[:, 0, :], NO[:, 4, :], 0.0, ALU.add, ALU.add), t, tz)
        t_bs = tt(NO[:, 2, :], NO[:, 1, :], NO[:, 0, :], ALU.subtract, t_in)
        t = tt(NO[:, 3, :], NO[:, 2, :], EJ, ALU.subtract, t_bs)
        t_of = ts(NO[:, 3, :], NO[:, 3, :], float(CAP), float((NE - 1) * CAP), ALU.mult, ALU.add, t)
        SF = sb([P, 2, TB])
        t_sl = []
        for k in range(2):
            t = None
            for i, m in enumerate((RK[:, 0:128].rearrange("p (t n) -> p t n", t=TB), bt(EJ, 32), bt(NO[:, 3, :], 32))):
                t = tt(W32[:, :, :], OH[k][:, :, :], m, ALU.mult, t_oh, t_rk, t_of, t, t_sl)
                t = red(sx(9 + i), W32[:, :, :], ALU.add, t)
            t = stt(sx(12), sx(9), float(CAP), sx(11), ALU.is_ge, ALU.mult, t)
            t = stt(sx(13), sx(10), float(CAP), sx(9), ALU.mult, ALU.add, t)
            t_sl.append(tt(SF[:, k, :], sx(12), sx(13), ALU.add, t))
        SL = SLK
        t_sli = V(lambda e: e.tensor_copy(SL[:, :, :], SF[:, :, :]), t_sl)
        IE = sb([1, NOVF, 32])
        IF_ = sb([1, NOVF, 32])
        CV = sb([1, 8])
        t_cv = []
        for n in range(NOVF):
            t = ts(IE[:, n, :], NO[0:1, 1, :], float(n), None, ALU.is_gt, None, t_in)
            t = stt(IE[:, n, :], NO[0:1, 2, :], float(n), IE[:, n, :], ALU.is_le, ALU.mult, t, t_bs)
            t_cv.append(tt(IF_[:, n, :], IE[:, n, :], CJ[0:1, 36:68], ALU.mult, t))
        t = red(CV[:, 0:NOVF], IF_[:, :, :], ALU.add, t_cv)
        t = ts(CV[:, 7:8], NO[0:1, 1, 31:32], -1.0, float(NOVF), ALU.mult, ALU.add, t)
        t_ct = V(lambda e: e.tensor_copy(CT[:, :], CV[:, :]), t)
        ZT = sb([NBLK, P])
        t = V(lambda e: e.memset(ZT[:, :], 0.0))
        t_z = K.dma("scalar", "zt", st_d.rearrange("(b s) o -> b (s o)", s=CAP), ZT[:, :], t)
        t_st = []
        for k in range(2):
            for tb in range(TB):
                t_st.append(K.gather("st", st_d, SL[:, k, tb:tb + 1], CJ[:, 68 + tb:69 + tb], None, t_sli, t_z))
        TT_ = sb([NBLK, P])
        t = K.dma("sync", "tt", TT_[:, :], st_d.rearrange("(b s) o -> b (s o)", s=CAP), t_st)
        b = bank()
        tm = PE(lambda e, b=b: e.transpose(banks[b][:, 0:NBLK], TT_[:, :], ident[0:NBLK, 0:NBLK]), t, bfree[b])
        t_tok = V(lambda e, b=b: e.tensor_copy(TOK[:, :], banks[b][:, 0:NBLK]), tm)
        bfree[b] = [t_tok]
        pop()
        ft = pop()
        add_raw(3, ft)
        add_split(1, ft)

        push()
        XT = [[sb([P, KC, P], F32R), sb([P, KC, P], F32R)] for _ in range(2)]
        SG = [sb([P, DE]) for _ in range(2)]
        GM = sb([P, DE])
        GTs = [sb([P, TB, P], F32R), sb([P, TB, P], F32R)]
        YB = [sb([P, D]) for _ in range(2)]
        xg_free = [[t_xd] for _ in range(4)]
        xt_free = [[], []]
        sg_free = [[], []]
        gm_free, gt_free = [], []
        yb_free = [[], []]
        t_xg = {}

        def fetch(n):
            if n < NE and n not in t_xg:
                t_xg[n] = K.gather(f"xg{n % 4}", XN[:, n % 4, :], None, xn_d, TOK[:, n:n + 1],
                                   t_tok, t_xd, xg_free[n % 4], ft)

        def turn_x(n):
            z = n % 2
            toks = []
            for half in range(2):
                b = bank()
                for k in range(4):
                    kc = 4 * half + k
                    tm = PE(lambda e, b=b, k=k, kc=kc, n=n: e.transpose(banks[b][:, k * P:(k + 1) * P],
                                                                       XN[:, n % 4, kc * P:(kc + 1) * P],
                                                                       ident[:, :]), t_xg[n], bfree[b])
                v = banks[b][:, :].rearrange("p (c n) -> p c n", c=4)
                hi, lo = (XT[z][i][:, 4 * half:4 * half + 4, :] for i in (0, 1))
                th = act(hi, v, ACT.Copy, tm, xt_free[z])
                tl = tt(lo, v, hi.bitcast(F32), ALU.subtract, th, xt_free[z])
                bfree[b] = [tl]
                toks += [th, tl]
            xg_free[n % 4] = [tm]
            return toks

        for n in range(3):
            fetch(n)
        t_xt = {0: turn_x(0)}
        t_yd = []
        for n in range(NE):
            z = n % 2
            fetch(n + 3)
            ab = []
            for m in range(2):
                b = bank()
                for q in range(2):
                    w = take()
                    for k in range(4):
                        kc = 4 * q + k
                        tm = mm3(banks[b][:, :], [XT[z][i][:, kc, :] for i in (0, 1)], [w[i][:, k, :] for i in (0, 1)],
                                 kc == 0, kc == KC - 1, w[2], t_xt[n], bfree[b] if kc == 0 else None)
                    done(w, tm)
                ab.append(b)
                if m == 0:
                    t_sg = act(SG[z][:, :], banks[b][:, :], ACT.Silu, tm, sg_free[z])
                    bfree[b] = [t_sg]
            xt_free[z] = [tm]
            t_gm = tt(GM[:, :], SG[z][:, :], banks[ab[1]][:, :], ALU.mult, tm, t_sg, gm_free)
            bfree[ab[1]] = [t_gm]
            sg_free[z] = [t_gm]
            if n + 1 < NE:
                t_xt[n + 1] = turn_x(n + 1)
            b = bank()
            for k in range(4):
                tm = PE(lambda e, b=b, k=k: e.transpose(banks[b][:, k * P:(k + 1) * P], GM[:, k * P:(k + 1) * P],
                                                       ident[:, :]), t_gm, bfree[b])
            gm_free = [tm]
            v = banks[b][:, :].rearrange("p (c n) -> p c n", c=4)
            th = act(GTs[0][:, :, :], v, ACT.Copy, tm, gt_free)
            tl = tt(GTs[1][:, :, :], v, GTs[0][:, :, :].bitcast(F32), ALU.subtract, th, gt_free)
            bfree[b] = [tl]
            by = [bank(), bank()]
            ty = [None, None]
            for q in range(2):
                w = take()
                for hh in range(2):
                    for k in range(2):
                        kc = 2 * q + k
                        ty[hh] = mm3(banks[by[hh]][:, :], [GTs[i][:, kc, :] for i in (0, 1)],
                                     [w[i][:, k, hh * 512:(hh + 1) * 512] for i in (0, 1)],
                                     kc == 0, kc == 3, w[2], th, tl, bfree[by[hh]] if kc == 0 else None)
                done(w, ty[1])
            gt_free = [ty[1]]
            tc = []
            for hh in range(2):
                hs = slice(hh * 512, (hh + 1) * 512)
                t = act(YB[z][:, hs], banks[by[hh]][:, :], ACT.Copy, ty[hh], yb_free[z])
                bfree[by[hh]] = [t]
                tc.append(t)
            t = K.dma("scalar", f"yd{z}", y_d[n * CAP:(n + 1) * CAP, :], YB[z][:, :], tc)
            yb_free[z] = [t]
        t_yd = [yb_free[0], yb_free[1]]
        ft = pop()

        push()
        RWt = [sb([P, 4, DE]) for _ in range(2)]
        XO = sb([P, KC, P])
        SO_ = sb([P, DE])
        GO = sb([P, TB, P])
        YO = sb([P, D])
        before = dict(K.last)
        for n in range(NOVF):
            K.enter(CT[0:1, 7:8], NOVF - n, t_ct, ft, t_yz, t_yd)
            if n == 0:
                K.part = "more"
                rw_t = [None, None]
                wn = 0
                t_y = None
                prev = {}
            t_xgo = K.gather("xgo", XN[:, 0, :], None, xn_d, TOK[:, NE + n:NE + n + 1], t_tok, prev.get("xt"))
            t = None
            for half in range(2):
                for k in range(4):
                    kc = 4 * half + k
                    tm = PE(lambda e, k=k, kc=kc, half=half: e.transpose(banks[half][:, k * P:(k + 1) * P],
                                                                        XN[:, 0, kc * P:(kc + 1) * P],
                                                                        ident[:, :]), t_xgo, prev.get("xe"))
            t_xe = []
            for half in range(2):
                v = banks[half][:, :].rearrange("p (c n) -> p c n", c=4)
                t_xe.append(V(lambda e, v=v, half=half: e.tensor_copy(XO[:, 4 * half:4 * half + 4, :], v),
                              tm, prev.get("ab")))
            prev["xt"], prev["xe"] = tm, t_xe
            for m in range(2):
                for q in range(2):
                    i = wn % 2
                    wn += 1
                    tw = K.dma_from("more_w%d" % i, RWt[i][:, :, :], n,
                                    lambda v, m=m, q=q: g[("w_expert_gate", "w_expert_up")[m]][0][bass.ds(v, 1), :, :]
                                    .rearrange("a (c p) n -> p (a c) n", p=P)[:, 4 * q:4 * q + 4, :], rw_t[i])
                    for k in range(4):
                        kc = 4 * q + k
                        tm = mm(banks[2 + m][:, :], XO[:, kc, :], RWt[i][:, k, :], kc == 0, kc == KC - 1,
                                tw, t_xe, prev.get("g") if kc == 0 else None)
                    rw_t[i] = tm
            prev["ab"] = tm
            t = act(SO_[:, :], banks[2][:, :], ACT.Silu, tm, prev.get("gt"))
            t = tt(SO_[:, :], SO_[:, :], banks[3][:, :], ALU.mult, t, tm)
            prev["g"] = t
            for k in range(4):
                tm = PE(lambda e, k=k: e.transpose(banks[4][:, k * P:(k + 1) * P], SO_[:, k * P:(k + 1) * P],
                                                  ident[:, :]), t, prev.get("go"))
            prev["gt"] = tm
            t_go = V(lambda e: e.tensor_copy(GO[:, :, :], banks[4][:, :].rearrange("p (c n) -> p c n", c=4)),
                     tm, prev.get("dn"))
            prev["go"] = t_go
            for q in range(2):
                i = wn % 2
                wn += 1
                tw = K.dma_from("more_w%d" % i, RWt[i][:, :, :].rearrange("p (a b) n -> p a (b n)", a=2), n,
                                lambda v, q=q: g["w_expert_down"][0][bass.ds(v, 1), :, :]
                                .rearrange("a (c p) n -> p (a c) n", p=P)[:, 2 * q:2 * q + 2, :], rw_t[i])
                for hh in range(2):
                    for k in range(2):
                        kc = 2 * q + k
                        tm = mm(banks[5 + hh][:, :], GO[:, kc, :], RWt[i][:, 2 * k + hh, :], kc == 0, kc == 3,
                                tw, t_go, prev.get("yo") if kc == 0 else None)
                rw_t[i] = tm
            prev["dn"] = tm
            tc = [V(lambda e, hh=hh: e.tensor_copy(YO[:, hh * 512:(hh + 1) * 512], banks[5 + hh][:, :]), tm, t_y)
                  for hh in range(2)]
            prev["yo"] = tc
            t_y = K.dma("scalar", "more_y", y_d[(NE + n) * CAP:(NE + n + 1) * CAP, :], YO[:, :], tc)
            for e in K.q:
                K.wait(e, t_y)
        for n in range(NOVF):
            K.leave()
        K.part = "main"
        K.last = before
        t_join = A(lambda e: e.activation(small[:, 40:41], small[:, 32:33], ACT.Copy), t_gt)
        ft = [pop(), t_join]

        push()
        FGb = sb([P, D])
        Y2 = [[sb([P, D]), sb([P, D])] for _ in range(2)]
        t_fg = K.dma("scalar", "fg", FGb[:, :], g["final_g"].partition_broadcast(P), ft)
        y_free = [[ft], [ft]]
        t_x = []
        for tb in range(TB):
            z = tb % 2
            ty = [K.gather(f"y{z}{k}", Y2[z][k][:, :], None, y_d, SLK[:, k, tb:tb + 1], t_yd, t_join, y_free[z])
                  for k in range(2)]
            t = ts(Y2[z][0][:, :], Y2[z][0][:, :], small[:, 32 + tb:33 + tb], None, ALU.mult, None, ty, t_gt)
            t = stt(Y2[z][0][:, :], Y2[z][1][:, :], small[:, 36 + tb:37 + tb], Y2[z][0][:, :], ALU.mult, ALU.add, t)
            t = tt(Y2[z][0][:, :], Y2[z][0][:, :], GF[:, :], ALU.mult, t, t_mod[5])
            t = tt(X[:, tb, :], X[:, tb, :], Y2[z][0][:, :], ALU.add, t)
            y_free[z] = [t]
            t_x.append(t)
        t_xn = normalize(t_x)
        t_x = [tt(X[:, tb, :], XN[:, tb, :], FGb[:, :], ALU.mult, t_xn, t_fg) for tb in range(TB)]
        pop()

        push()
        UT = sb([P, KC, T])
        BSP = GF[:, :].rearrange("p (g t) -> p g t", g=8)
        WSN = [z[:, :].rearrange("p (g s) -> p g s", g=4) for z in tmpT]
        WSs = [sb([P, 8, P], F32R), sb([P, 8, P], F32R)]
        t_bsp = K.dma("scalar", "bsp", GF[:, :],
                      g["a_b_sp_2"][0].rearrange("g t -> (g t)").partition_broadcast(P), ft, t_x)
        t_ws = []
        for q in range(2):
            t = K.dma("scalar", f"wsn{q}", WSN[q], g["a_w_sp_2"][0, 4 * q:4 * q + 4].rearrange("g t s -> t g s"),
                      ft, tmp_free[q])
            t = G(lambda e, q=q: e.affine_select(out=WSN[q], in_=WSN[q], compare_op=ALU.is_ge, fill=0.0,
                                                 base=0, pattern=[[0, 4], [-1, P]], channel_multiplier=1), t)
            b = bank()
            for k in range(4):
                tm = PE(lambda e, b=b, k=k, q=q: e.transpose(banks[b][:, k * P:(k + 1) * P], WSN[q][:, k, :],
                                                            ident[:, :]), t, bfree[b])
            tmp_free[q] = [tm]
            v = banks[b][:, :].rearrange("p (c n) -> p c n", c=4)
            hi, lo = (WSs[i][:, 4 * q:4 * q + 4, :] for i in (0, 1))
            th = act(hi, v, ACT.Copy, tm)
            tl = tt(lo, v, hi.bitcast(F32), ALU.subtract, th)
            bfree[b] = [tl]
            t_ws += [th, tl]
        push()
        hTh = [sb([P, KC, T], F32R), sb([P, KC, T], F32R)]
        t_xn = normalize(t_x)
        t_h = to_features(hTh, t_xn, lambda kc: col("an", kc), None)
        t_ut = []
        for i, (b, tm) in enumerate(t_blocks(hTh, t_h, 4)):
            t = act(UT[:, i, :], banks[b][:, :], ACT.Gelu_apprx_tanh, tm)
            bfree[b] = [t]
            t_ut.append(t)
        t_v = [[] for _ in range(TB)]
        for h in range(2):
            for tb, (b, tm) in enumerate(n_blocks(hTh, t_h, KC)):
                t = act(XN[:, tb, h * 512:(h + 1) * 512], banks[b][:, :], ACT.Gelu_apprx_tanh, tm, t_h,
                        accum_out=small[:, 2 * tb + h:2 * tb + h + 1])
                bfree[b] = [t]
                t_v[tb].append(t)
        sm = small[:, 0:8].rearrange("p (t h) -> p t h", h=2)
        t = tt(small[:, 8:12], sm[:, :, 0], sm[:, :, 1], ALU.add, t_v)
        t = ts(small[:, 8:12], small[:, 8:12], 1.0 / D, None, ALU.mult, None, t)
        tc = [ts(XN[:, tb, :], XN[:, tb, :], small[:, 8 + tb:9 + tb], None, ALU.subtract, None, t) for tb in range(TB)]
        tq, jf = [], []
        for tb in range(TB):
            for h in range(2):
                tq.append(act(tmpT[h][:, :], XN[:, tb, h * 512:(h + 1) * 512], ACT.Square, tc, tmp_free, tq[-2:-1],
                              accum_out=small[:, 2 * tb + h:2 * tb + h + 1]))
        tmp_free[0] = tmp_free[1] = [tq]
        t = tt(small[:, 8:12], sm[:, :, 0], sm[:, :, 1], ALU.add, tq)
        t = act(small[:, 8:12], small[:, 8:12], ACT.Sqrt, t, scale=1.0 / D, bias=epst[:, 0:1])
        t = V(lambda e: e.reciprocal(small[:, 8:12], small[:, 8:12]), t)
        t_v = [ts(XN[:, tb, :], XN[:, tb, :], small[:, 8 + tb:9 + tb], None, ALU.mult, None, t) for tb in range(TB)]
        mixT = hTh
        t_hfree = tm
        Vh = [[sb([P, TB, P], F32R), sb([P, TB, P], F32R)] for _ in range(2)]
        vh_free = [[], []]
        toks = []
        pend = []
        for gi in range(8):
            z = gi % 2
            tv = split(Vh[z][0][:, :, :], Vh[z][1][:, :, :], XN[:, :, gi * P:(gi + 1) * P], t_v, vh_free[z])
            b = bank()
            for tb in range(TB):
                tm = mm3(banks[b][:, tb * P:(tb + 1) * P], [Vh[z][i][:, tb, :] for i in (0, 1)],
                         [WSs[i][:, gi, :] for i in (0, 1)], True, True, tv, t_ws, bfree[b])
            vh_free[z] = [tm]
            i = tmp_turn[0] % 2
            tmp_turn[0] += 1
            t = stt(tmpT[i][:, :].rearrange("p (a c) -> p a c", a=4), banks[b][:, :].rearrange("p (a c) -> p a c", a=4),
                    col("av", gi), BSP[:, gi, :].unsqueeze(1).broadcast_to([P, 4, P]), ALU.mult, ALU.add,
                    tm, t_bsp, tmp_free[i])
            bfree[b] = [t]
            t = tt(tmpT[i][:, :], tmpT[i][:, :], UT[:, gi, :], ALU.mult, t, t_ut)
            tmp_free[i] = split(mixT[0][:, gi, :], mixT[1][:, gi, :], tmpT[i][:, :], t, t_hfree)
            toks += tmp_free[i]
        t_x = add_to_x(mixT, toks, KC)
        pop()
        pop()

        def ffn(l, t_x):
            push()
            hTh = [sb([P, KC, T], F32R), sb([P, KC, T], F32R)]
            AT = [sb([P, 8, T], F32R), sb([P, 8, T], F32R)]
            SB_ = tmpT
            t_xn = normalize(t_x)
            t_h = to_features(hTh, t_xn, lambda kc: col("fn", 8 * l + kc), None)
            at_free = []
            sb_free = tmp_free
            t_x = None
            for f0, fn in FG:
                toks = []
                for f in range(0, fn, 2):
                    gs = []
                    for j, (b, tm) in enumerate(t_blocks(hTh, t_h, 1)):
                        t = act(SB_[j][:, :], banks[b][:, :], ACT.Silu, tm, sb_free[j])
                        bfree[b] = [t]
                        gs.append(t)
                    for j, (b, tm) in enumerate(t_blocks(hTh, t_h, 1)):
                        t = tt(SB_[j][:, :], SB_[j][:, :], banks[b][:, :], ALU.mult, tm, gs[j])
                        bfree[b] = [t]
                        sb_free[j] = split(AT[0][:, f + j, :], AT[1][:, f + j, :], SB_[j][:, :], t, at_free)
                        toks += sb_free[j]
                t_x = add_to_x(AT, toks, fn)
                at_free = [K.last["tensor"]]
            pop()
            return t_x

        t_x = ffn(0, t_x)

        push()
        QO = sb([P, 8, T])
        KF = sb([P, 8, T])
        push()
        hTh = [sb([P, KC, T], F32R), sb([P, KC, T], F32R)]
        t_xn = normalize(t_x)
        t_h = to_features(hTh, t_xn, lambda kc: col("bn", kc), None)
        t_q = []
        for i, (b, tm) in enumerate(t_blocks(hTh, t_h, 4)):
            t = act(QO[:, i, :], banks[b][:, :], ACT.Copy, tm)
            bfree[b] = [t]
            t_q.append(t)
        K.wait("scalar", tm)
        K.wait("vector", tm)
        t_h = to_features(hTh, t_xn, lambda kc: col("kvn", kc), None)
        t_v = []
        for h in range(2):
            for tb, (b, tm) in enumerate(n_blocks(hTh, t_h, KC)):
                t = act(XN[:, tb, h * 512:(h + 1) * 512], banks[b][:, :], ACT.Copy, tm, t_h)
                bfree[b] = [t]
                t_v.append(t)
        t_k = []
        for i, (b, tm) in enumerate(t_blocks(hTh, t_h, 4)):
            t = act(KF[:, i, :], banks[b][:, :], ACT.Copy, tm)
            bfree[b] = [t]
            t_k.append(t)
        pop()
        push()
        LAM = tmpT[0][:, 0:256].rearrange("p (a d) -> p a d", a=4)
        AB, NDf = GF[:, 0:T], GF[:, T:D]
        P0 = [sb([P, 1280]) for _ in range(2)]
        P1 = [sb([P, T]) for _ in range(2)]
        NDi = P1[0][:, :].bitcast(I32)
        Qs = [sb([P, T], F32R), sb([P, T], F32R)]
        Ks = [sb([P, T], F32R), sb([P, T], F32R)]
        Vs = [sb([P, TB, P], F32R), sb([P, TB, P], F32R)]
        AH = [[sb([P, T], F32R), sb([P, T], F32R)] for _ in range(2)]
        t_lm = K.dma("scalar", "lam", tmpT[0][:, 0:256],
                     g["b_lambda_2"][0].rearrange("a d -> (a d)").partition_broadcast(P), tmp_free[0])
        ls = small[:, 48:56]
        t = tt(LAM[:, 0, :], LAM[:, 0, :], LAM[:, 1, :], ALU.mult, t_lm)
        t = tt(LAM[:, 2, :], LAM[:, 2, :], LAM[:, 3, :], ALU.mult, t)
        t = V(lambda e: e.tensor_reduce(ls[:, 0:1], LAM[:, 0, :], AX, ALU.add), t)
        t = V(lambda e: e.tensor_reduce(ls[:, 1:2], LAM[:, 2, :], AX, ALU.add), t)
        tmp_free[0] = [t]
        t = act(ls[:, 2:4], ls[:, 0:2], ACT.Exp, t)
        t = tt(ls[:, 4:5], ls[:, 3:4], ls[:, 2:3], ALU.subtract, t)
        t_nl = ts(ls[:, 5:6], ls[:, 4:5], -LAMBDA_INIT, None, ALU.add, None, t)
        t_sb = ts(ls[:, 6:7], col("sub", 0), 1.0 - LAMBDA_INIT, None, ALU.mult, None, t_vt)
        t = G(lambda e: e.iota(NDi, pattern=[[1, T]], base=-384, channel_multiplier=-1))
        t = V(lambda e: e.tensor_copy(NDf, NDi), t)
        t_nd = G(lambda e: e.affine_select(out=NDf, in_=NDf, compare_op=ALU.is_ge, fill=-BIG, base=384,
                                           pattern=[[-1, T]], channel_multiplier=1), t)
        off = [0, 128, 384, 768]
        p0_free, p1_free = [[], []], [[t_nd], [t_nd]]
        ab_free, qk_free, v_free = [], [], []
        ah_free = [[], []]
        st = small[:, 0:16]
        t_o = []

        def scores(h):
            nonlocal ab_free, qk_free
            z = h % 2
            slope = 2.0 ** (-(h + 1))
            t_ab = ts(AB, NDf, slope * 8.0, None, ALU.mult, None, t_nd, ab_free)
            tq = split(Qs[0][:, :], Qs[1][:, :], QO[:, h, :], t_q, qk_free)
            tk = split(Ks[0][:, :], Ks[1][:, :], KF[:, h, :], t_k, qk_free)
            te = []
            last_e = None
            for tb in range(TB):
                n = (tb + 1) * P
                for m in range(2):
                    pr = slice(64 * m, 64 * m + 64)
                    pt = P0[z][:, off[tb]:off[tb] + n] if m == 0 else P1[tb % 2][:, 0:n]
                    b = bank()
                    tm = mm3(banks[b][:, 0:n], [Qs[i][pr, tb * P:(tb + 1) * P] for i in (0, 1)],
                             [Ks[i][pr, 0:n] for i in (0, 1)], True, True, tq, tk, bfree[b])
                    mx = st[:, 4 * m:4 * m + 1]
                    fr = p0_free[z] if m == 0 else p1_free[tb % 2]
                    t = V(lambda e, b=b, pt=pt, n=n, tb=tb, mx=mx: e.tensor_tensor_reduce(
                        out=pt, in0=banks[b][:, 0:n], in1=AB[:, 384 - tb * P:512], scale=1.0, scalar=-3.0e38,
                        op0=ALU.add, op1=ALU.max, accum_out=mx), tm, t_ab, fr, last_e)
                    bfree[b] = [t]
                    t = ts(st[:, 4 * m + 1:4 * m + 2], mx, -0.125, None, ALU.mult, None, t, last_e)
                    t = act(pt, pt, ACT.Exp, t, scale=0.125, bias=st[:, 4 * m + 1:4 * m + 2],
                            accum_out=st[:, 4 * m + 2:4 * m + 3])
                    te.append(t)
                    if m == 0:
                        t_e0 = t
                r0, r1 = st[:, 3:4], st[:, 7:8]
                ta = V(lambda e: e.reciprocal(r0, st[:, 2:3]), t_e0, last_e)
                tb_ = V(lambda e: e.reciprocal(r1, st[:, 6:7]), t, last_e)
                tb_ = tt(r1, r1, ls[:, 5:6], ALU.mult, tb_, t_nl)
                a0, a1 = P0[z][:, off[tb]:off[tb] + n], P1[tb % 2][:, 0:n]
                t = ts(a0, a0, r0, None, ALU.mult, None, ta, t_e0)
                last_e = stt(a0, a1, r1, a0, ALU.mult, ALU.add, t, tb_)
                te.append(last_e)
                p1_free[tb % 2] = [last_e]
            ab_free = [last_e]
            qk_free = [tm]
            return te, last_e

        def values(h, t_a):
            nonlocal v_free
            z = h % 2
            tv = split(Vs[0][:, :, :], Vs[1][:, :, :], XN[:, :, h * P:(h + 1) * P], t_v, v_free)
            bo = None
            for s in range(TB):
                y = s % 2
                n = T - s * P
                b = bank()
                for tb in range(s, TB):
                    tm = PE(lambda e, b=b, s=s, tb=tb: e.transpose(
                        banks[b][:, (tb - s) * P:(tb - s + 1) * P],
                        P0[z][:, off[tb] + s * P:off[tb] + (s + 1) * P], ident[:, :]), t_a, bfree[b])
                if s == 3:
                    p0_free[z] = [tm]
                th = act(AH[y][0][:, 0:n], banks[b][:, 0:n], ACT.Copy, tm, ah_free[y])
                tl = tt(AH[y][1][:, 0:n], banks[b][:, 0:n], AH[y][0][:, 0:n].bitcast(F32), ALU.subtract,
                        th, ah_free[y])
                bfree[b] = [tl]
                if bo is None:
                    bo = bank()
                tm = mm3(banks[bo][:, s * P:T], [Vs[i][:, s, :] for i in (0, 1)], [AH[y][i][:, 0:n] for i in (0, 1)],
                         s == 0, s == 3, tv, th, tl, bfree[bo] if s == 0 else None)
                ah_free[y] = [tm]
            v_free = [tm]
            i = tmp_turn[0] % 2
            tmp_turn[0] += 1
            o = QO[:, h, :]
            to = V(lambda e, bo=bo, o=o: e.tensor_copy(o, banks[bo][:, :]), tm, qk_free, t_a)
            bfree[bo] = [to]
            t = act(tmpT[i][:, :], o, ACT.Square, to, tmp_free[i])
            b = bank()
            tm = mm(banks[b][:, :], onesf[:, :], tmpT[i][:, :], True, True, t, bfree[b])
            t = act(tmpT[i][:, :], banks[b][:, :], ACT.Sqrt, tm, scale=1.0 / P, bias=epst[:, 0:1])
            bfree[b] = [t]
            t = V(lambda e, i=i: e.reciprocal(tmpT[i][:, :], tmpT[i][:, :]), t)
            t = stt(o, o, ls[:, 6:7], tmpT[i][:, :], ALU.mult, ALU.mult, t, t_sb, to)
            tmp_free[i] = [t]
            t_o.append(t)

        prev_a = None
        for h in range(9):
            if h < 8:
                te, _ = scores(h)
            if h > 0:
                values(h - 1, prev_a)
            prev_a = te
        pop()
        push()
        mixT = [sb([P, KC, T], F32R), sb([P, KC, T], F32R)]
        toks = [split(mixT[0][:, h, :], mixT[1][:, h, :], QO[:, h, :], t_o[h]) for h in range(8)]
        t_x = add_to_x(mixT, toks, KC)
        pop()
        pop()
        t_x = ffn(1, t_x)
        push()
        FGb = sb([P, D])
        t_fg = K.dma("scalar", "fg", FGb[:, :], g["final_norm_2"].partition_broadcast(P), K.last["scalar"])
        t_xn = normalize(t_x)
        t_x = [tt(X[:, tb, :], XN[:, tb, :], FGb[:, :], ALU.mult, t_xn, t_fg) for tb in range(TB)]
        finish_x(t_x)


_INS = ['x', 'c', 'ada_w', 'ada_b', 'norm1_g', 'w_in', 'conv_w', 'conv_b', 'w_q', 'w_k', 'b_igate', 'b_fgate',
        'mlstm_norm_g', 'mlstm_skip', 'w_pool', 'b_pool', 'pool_scale', 'w_out', 'norm2_g', 'w_router_group',
        'b_router_group', 'w_router_expert', 'b_router_expert', 'w_expert_gate', 'w_expert_up', 'w_expert_down',
        'final_g', 'a_norm_2', 'a_w_in_2', 'a_v_norm_2', 'a_w_sp_2', 'a_b_sp_2', 'a_w_out_2', 'ffn_norm_2',
        'ffn_w_gu_2', 'ffn_w_down_2', 'kv_norm_2', 'kv_w_2', 'b_norm_2', 'b_w_q_2', 'b_lambda_2', 'b_subln_2',
        'b_w_o_2', 'final_norm_2']


def kernel(**inputs):
    import numpy as np
    import concourse.bacc as bacc
    from concourse.bass_utils import run_bass_kernel_spmd

    nc = bacc.Bacc("TRN2", target_bir_lowering=False, num_devices=1)
    arrays, g = {}, {}
    for name in _INS:
        a = np.ascontiguousarray(inputs[name])
        arrays[f"in_{name}"] = a
        g[name] = nc.dram_tensor(f"in_{name}", a.shape, mybir.dt.from_np(a.dtype), kind="ExternalInput").ap()
    out = nc.dram_tensor("out_x", (1, T, D), F32, kind="ExternalOutput").ap()
    program(nc, g, out)
    r = run_bass_kernel_spmd(nc, [arrays], core_ids=[0])
    return r.results[0]["out_x"]
```

```python
from collections import deque
from contextlib import ExitStack
import math

import concourse.bass as bass
from concourse import mybir

F32 = mybir.dt.float32
F32R = mybir.dt.float32r
I32 = mybir.dt.int32
ALU = mybir.AluOpType
ACT = mybir.ActivationFunctionType
AX = mybir.AxisListType.X

P = 128
D = 1024
T = 512
TB = 4
KC = 8
NE = 32
DE = 512
CAP = 128
NOVF = 7
NBLK = NE + NOVF
DFF = 2816
FB = DFF // P
EPS = 1e-6
BIG = 1e30
SLOT = 2048
LAMBDA_INIT = 0.8 - 0.6 * math.exp(-0.3)


class Tok:

    def __init__(self, sem, val=None):
        self.sem, self.val, self.used = sem, val, val is not None


def flat(xs):
    for x in xs:
        if x is None:
            continue
        if isinstance(x, (list, tuple)):
            yield from flat(x)
        else:
            yield x


class Queues:

    def __init__(self, nc, ctx):
        self.nc, self.ctx = nc, ctx
        self.q = {n: [] for n in ("sync", "tensor", "vector", "scalar", "gpsimd")}
        self.sems = {}
        self.part = "main"
        self.last = {}
        self.experts = {}

    def sem(self, name):
        if name not in self.sems:
            self.sems[name] = [self.ctx.enter_context(self.nc.semaphore(name)), 0]
        return self.sems[name]

    def op(self, eng, fn, *after):
        t = Tok(self.sem(f"{self.part}_{eng}"))
        w = list(flat(after))
        for x in w:
            x.used = True
        self.q[eng].append(("op", fn, w, t))
        self.last[eng] = t
        return t

    def dma(self, eng, name, out, in_, *after):
        s = self.sem(name)
        s[1] += 16
        t = Tok(s, s[1])
        w = list(flat(after))
        for x in w:
            x.used = True
        self.q[eng].append(("dma", lambda e: e.dma_start(out, in_), w, t))
        return t

    def gather(self, name, out, out_idx, in_, in_idx, *after):
        s = self.sem(name)
        s[1] += 16
        t = Tok(s, s[1])
        w = list(flat(after))
        for x in w:
            x.used = True
        oo = bass.IndirectOffsetOnAxis(ap=out_idx, axis=0) if out_idx is not None else None
        io = bass.IndirectOffsetOnAxis(ap=in_idx, axis=0) if in_idx is not None else None
        self.q["gpsimd"].append(("dma", lambda e: e.indirect_dma_start(out=out, out_offset=oo, in_=in_, in_offset=io), w, t))
        return t

    def dma_from(self, name, out, n, src, *after):
        s = self.sem(name)
        s[1] += 16
        t = Tok(s, s[1])
        w = list(flat(after))
        for x in w:
            x.used = True
        self.q["sync"].append(("dma", lambda e: e.dma_start(out, src(self.expert(e, n))), w, t))
        return t

    def expert(self, e, n):
        if n not in self.experts:
            r = e.alloc_register(f"expert{n}")
            e.reg_load(r, self.table[0:1, n:n + 1])
            self.experts[n] = e.snap(r, min_val=0, max_val=NE - 1)
        return self.experts[n]

    def wait(self, eng, *after):
        w = list(flat(after))
        for x in w:
            x.used = True
        self.q[eng].append(("wait", None, w, None))

    def enter(self, reg_ap, bound, *after):
        for e in self.q:
            self.wait(e, *after)
            self.q[e].append(("enter", (reg_ap, bound), [], None))

    def leave(self):
        for e in self.q:
            self.q[e].append(("leave", None, [], None))

    def fence(self):
        toks = [t for e, t in self.last.items() if e != "sync"]
        for e in ("tensor", "vector", "scalar", "gpsimd"):
            self.wait(e, toks)
        return toks

    def number(self):
        for items in self.q.values():
            for kind, _, _, t in items:
                if kind == "op" and t.used:
                    t.sem[1] += 1
                    t.val = t.sem[1]

    def run(self, name, eng):
        seen, saved, guards = {}, [], []
        for kind, fn, waits, t in self.q[name]:
            need = {}
            for w in waits:
                if need.get(id(w.sem), (0,))[0] < w.val:
                    need[id(w.sem)] = (w.val, w.sem[0])
            for k, (v, s) in need.items():
                if seen.get(k, 0) < v:
                    seen[k] = v
                    eng.wait_ge(s, v)
            if kind == "op":
                i = fn(eng)
                if t.used:
                    i.then_inc(t.sem[0], 1)
            elif kind == "dma":
                fn(eng).then_inc(t.sem[0], 16)
            elif kind == "enter":
                saved.append(dict(seen))
                r = eng.alloc_register(f"r_{name}_{len(self.q[name])}_{fn[1]}")
                eng.reg_load(r, fn[0])
                g = eng.If_lt(r, fn[1])
                g.__enter__()
                guards.append(g)
            elif kind == "leave":
                guards.pop().__exit__(None, None, None)
                seen = saved.pop()


def program(nc, g, out):
    ctx = ExitStack()
    with ctx:
        K = Queues(nc, ctx)
        scope = [ctx]
        cnt = [0]

        def sb(shape, dt=F32):
            cnt[0] += 1
            return scope[-1].enter_context(nc.sbuf_tensor(f"t{cnt[0]}", shape, dt))

        def push():
            s = ExitStack()
            scope.append(s)

        def pop():
            scope.pop().close()
            return K.fence()

        def V(fn, *a):
            return K.op("vector", fn, *a)

        def A(fn, *a):
            return K.op("scalar", fn, *a)

        def G(fn, *a):
            return K.op("gpsimd", fn, *a)

        def PE(fn, *a):
            return K.op("tensor", fn, *a)

        def act(out_, in_, func, *a, **kw):
            return A(lambda e: e.activation(out_, in_, func, **kw), *a)

        def tt(out_, x, y, op, *a):
            return V(lambda e: e.tensor_tensor(out_, x, y, op), *a)

        def gtt(out_, x, y, op, *a):
            return G(lambda e: e.tensor_tensor(out_, x, y, op), *a)

        def ts(out_, x, s1, s2, o1, o2, *a):
            if o2 is None:
                return V(lambda e: e.tensor_scalar(out_, x, s1, None, o1), *a)
            return V(lambda e: e.tensor_scalar(out_, x, s1, s2, o1, o2), *a)

        def stt(out_, x, s, y, o1, o2, *a):
            return V(lambda e: e.scalar_tensor_tensor(out=out_, in0=x, scalar=s, in1=y, op0=o1, op1=o2), *a)

        def mm(out_, l, r, start, stop, *a):
            return PE(lambda e: e.matmul(out_, l, r, start=start, stop=stop, skip_group_check=True), *a)

        def mm3(out_, l, r, start, stop, *a):
            mm(out_, l[0], r[0], start, False, *a)
            mm(out_, l[0], r[1], False, False)
            return mm(out_, l[1], r[0], False, stop)

        def split(hi, lo, x, *a):
            th = act(hi, x, ACT.Copy, *a)
            tl = tt(lo, x, hi.bitcast(F32), ALU.subtract, th, *a)
            return [th, tl]

        def finish_x(t_x):
            t = K.dma("scalar", "out", out.rearrange("a (t p) d -> p (a t) d", p=P), X[:, :, :], t_x)
            K.wait("scalar", t)
            K.wait("sync", [x[2] for x in loaded])
            while len(scope) > 1:
                scope.pop().close()
            K.number()
            block = ctx.enter_context(nc.Block())

            @block.sync
            def _(eng):
                K.run("sync", eng)

            @block.tensor
            def _(eng):
                K.run("tensor", eng)

            @block.vector
            def _(eng):
                K.run("vector", eng)

            @block.scalar
            def _(eng):
                K.run("scalar", eng)

            @block.gpsimd
            def _(eng):
                K.run("gpsimd", eng)

        banks = [ctx.enter_context(nc.psum_tensor(f"ps{i}", [P, 512], F32)) for i in range(8)]
        bank_turn = deque(range(8))

        class Banks(dict):

            def __setitem__(self, b, toks):
                dict.__setitem__(self, b, toks)
                bank_turn.append(b)

        bfree = Banks((b, []) for b in range(8))

        def bank():
            return bank_turn.popleft()

        X = sb([P, TB, D])
        XN = sb([P, TB, D])
        ident = sb([P, P])
        onesf = sb([P, P])
        onesr = sb([P, P], F32R)
        epst = sb([P, 1])
        VT = sb([P, P])
        tmpT = [sb([P, 512]) for _ in range(2)]
        small = sb([P, 64])

        t0 = G(lambda e: e.memset(ident[:, :], 0.0))
        t_id = G(lambda e: e.affine_select(out=ident[:, :], in_=ident[:, :], compare_op=ALU.not_equal, fill=1.0,
                                           base=0, pattern=[[-1, P]], channel_multiplier=1), t0)
        t_on = V(lambda e: e.memset(onesf[:, :], 1.0))
        t_one = tt(onesr[:, :], onesf[:, :], onesf[:, :], ALU.mult, t_on)
        t_eps = V(lambda e: e.memset(epst[:, :], EPS))
        xn_d = nc.dram_tensor("xn_d", [T, D], F32, kind="Internal").ap()
        y_d = nc.dram_tensor("y_d", [NBLK * CAP, D], F32, kind="Internal").ap()
        st_d = nc.dram_tensor("st_d", [NBLK * CAP, 1], F32, kind="Internal").ap()

        raws, splits = deque(), deque()

        def add_raw(n, *free):
            for _ in range(n):
                i = len(add_raw.all)
                add_raw.all.append(i)
                raws.append((sb([P, SLOT]), f"raw{i}", list(flat(free))))
        add_raw.all = []

        def add_split(n, *free):
            for _ in range(n):
                splits.append((sb([P, SLOT], F32R), sb([P, SLOT], F32R), list(flat(free))))

        items = []

        def t_item(w, n0):
            items.append(("w", w.rearrange("(c p) n -> p c n", p=P)[:, :, n0:n0 + 256], 8, 256))

        def n_item(w, k0, kn, n0, nn=512):
            items.append(("w", w.rearrange("(c p) n -> p c n", p=P)[:, k0:k0 + kn, n0:n0 + nn], kn, nn))

        ada = g["ada_w"][0].rearrange("(c p) n -> p c n", p=P)

        def ada_items(j):
            for c in range(4):
                items.append(("ada", ada[:, 2 * c:2 * c + 2, j * D:(j + 1) * D], (j, c), None))

        w_in = g["w_in"][0]
        ada_items(0)
        ada_items(1)
        main_items = items[:]
        items.clear()
        for n0 in (0, 256, 1544, 1544 + 256):
            t_item(w_in, n0)
        n_item(w_in, 0, 4, 512)
        n_item(w_in, 4, 4, 512)
        for n0 in (1024, 1280):
            t_item(w_in, n0)
        for h in (0, 512):
            for k in (4, 0):
                n_item(g["w_out"][0], k, 4, h)
        wi = items[:]
        items.clear()
        for j in (2, 3, 4, 5):
            ada_items(j)
        ai = items[:]
        items[:] = main_items + wi[0:2]
        for i in range(2, len(wi)):
            items += ai[2 * (i - 2):2 * (i - 1)]
            items.append(wi[i])
        for e in range(NE + 1):
            if e < NE:
                for k in (0, 4):
                    n_item(g["w_expert_gate"][0, e], k, 4, 0)
            if e > 0:
                for k in (0, 2):
                    n_item(g["w_expert_down"][0, e - 1], k, 2, 0, 1024)
            if e < NE:
                for k in (0, 4):
                    n_item(g["w_expert_up"][0, e], k, 4, 0)
        for h in (0, 512):
            for k in (0, 4):
                n_item(g["a_w_in_2"][0], k, 4, 1024 + h)
        for n0 in range(0, 1024, 256):
            t_item(g["a_w_in_2"][0], n0)
        for h in (0, 512):
            for k in (0, 4):
                n_item(g["a_w_out_2"][0], k, 4, h)
        FG = [(0, 8), (8, 8), (16, 6)]

        def ffn_items(l):
            for f0, fn in FG:
                for f in range(f0, f0 + fn, 2):
                    t_item(g["ffn_w_gu_2"][l], f * P)
                    t_item(g["ffn_w_gu_2"][l], DFF + f * P)
                for h in (0, 512):
                    for k in range(0, fn, 4):
                        n_item(g["ffn_w_down_2"][l], f0 + k, min(4, fn - k), h)

        ffn_items(0)
        for n0 in range(0, 1024, 256):
            t_item(g["b_w_q_2"][0], n0)
        for h in (0, 512):
            for k in (0, 4):
                n_item(g["kv_w_2"], k, 4, 1024 + h)
        for n0 in range(0, 1024, 256):
            t_item(g["kv_w_2"], n0)
        for h in (0, 512):
            for k in (0, 4):
                n_item(g["b_w_o_2"][0], k, 4, h)
        ffn_items(1)

        loaded = deque()
        ends = deque()
        ready = deque()
        nl = [0]
        npz = [0]

        def load_more():
            while raws and nl[0] < len(items):
                kind, ap, a_, b_ = items[nl[0]]
                ten, name, free = raws.popleft()
                n = ap.shape[1] * ap.shape[2]
                dst = ten[:, 0:n].rearrange("p (c n) -> p c n", c=ap.shape[1])
                t = K.dma("sync", name, dst, ap, free)
                loaded.append((ten, name, t))
                nl[0] += 1

        def prep_one(forced):
            if npz[0] >= len(items):
                return False
            kind, ap, a_, b_ = items[npz[0]]
            if kind == "ada" and not forced:
                return False
            if kind == "w" and not splits:
                return False
            load_more()
            ten, name, t = loaded.popleft()
            npz[0] += 1
            if kind == "ada":
                tl = ada_step(a_[0], a_[1], ten, t)
                raws.append((ten, name, [tl]))
            else:
                n = a_ * b_
                hi, lo, free = splits.popleft()
                tp = []
                for c in (slice(0, n // 2), slice(n // 2, n)):
                    th = act(hi[:, c], ten[:, c], ACT.Copy, t, free)
                    tl = tt(lo[:, c], ten[:, c], hi[:, c].bitcast(F32), ALU.subtract, th, free)
                    tp.append([th, tl])
                raws.append((ten, name, tp))
                v = lambda z: z[:, 0:n].rearrange("p (c n) -> p c n", c=a_)
                ready.append((v(hi), v(lo), tp, hi, lo))
            load_more()
            return True

        def take():
            while not ready:
                assert prep_one(True)
            w = ready.popleft()
            while ends:
                ends.popleft()()
            pump(2)
            while prep_one(False):
                pass
            return w

        def done(w, *toks):
            splits.append((w[3], w[4], list(flat(toks))))

        def pump(n):
            for _ in range(n):
                if npz[0] < len(items) and items[npz[0]][0] == "ada":
                    prep_one(True)

        GF = sb([P, D])
        RB = sb([P, 36])
        SLK = sb([P, 2, TB], I32)
        CT = sb([1, 8], I32)
        K.table = CT
        TOK = sb([P, NBLK], I32)
        add_raw(3)
        add_split(2)
        push()
        tri = sb([P, P])
        neg = sb([P, P])
        sel = sb([4, 4 * P])
        VR = sb([P, P])
        t0 = G(lambda e: e.memset(neg[:, :], 0.0))
        t_neg = G(lambda e: e.affine_select(out=neg[:, :], in_=neg[:, :], compare_op=ALU.is_ge, fill=-BIG,
                                            base=0, pattern=[[1, P]], channel_multiplier=-1), t0)
        t0 = G(lambda e: e.memset(sel[:, :], 0.0))
        sv = sel[:, :].rearrange("k (h p) -> k h p", h=4)
        t_sel = G(lambda e: e.affine_select(out=sv, in_=sv, compare_op=ALU.not_equal, fill=1.0,
                                            base=0, pattern=[[1, 4], [0, P]], channel_multiplier=-1), t0)
        t0 = G(lambda e: e.memset(tri[:, :], 1.0))
        t_tri = G(lambda e: e.affine_select(out=tri[:, :], in_=tri[:, :], compare_op=ALU.is_gt, fill=0.0,
                                            base=0, pattern=[[1, P]], channel_multiplier=-1), t0)

        vec = {}
        row = 0
        t_vr = []
        for name, ap, n in (
            ("c", g["c"], 8), ("n1", g["norm1_g"], 8), ("an", g["a_norm_2"], 8), ("fn", g["ffn_norm_2"], 16),
            ("kvn", g["kv_norm_2"], 8), ("bn", g["b_norm_2"], 8), ("cw", g["conv_w"], 16), ("cb", g["conv_b"], 4),
            ("mn", g["mlstm_norm_g"], 4), ("sk", g["mlstm_skip"], 4), ("bp", g["b_pool"], 4),
            ("psc", g["pool_scale"], 4), ("av", g["a_v_norm_2"], 8), ("sub", g["b_subln_2"], 1),
        ):
            ap = ap.rearrange({1: "(r p) -> r p", 2: "a (r p) -> (a r) p", 3: "a b (r p) -> (a b r) p"}[len(ap.shape)], p=P)
            t_vr.append(K.dma("scalar", "vr", VR[row:row + n, :], ap))
            vec[name] = row
            row += n
        NV = row
        t_x = [K.dma("scalar", "x", X[:, :, :], g["x"].rearrange("a (t p) d -> p (a t) d", p=P))] * TB
        b = bank()
        t0 = PE(lambda e, b=b: e.transpose(banks[b][:, 0:NV], VR[0:NV, :], ident[0:NV, 0:NV]), t_vr, t_id)
        t_vt = V(lambda e, b=b: e.tensor_copy(VT[:, 0:NV], banks[b][:, 0:NV]), t0)
        bfree[b] = [t_vt]

        def col(name, i):
            return VT[:, vec[name] + i:vec[name] + i + 1]

        GA, G2, S2 = sb([P, D]), sb([P, D]), sb([P, D])
        acc = [sb([P, D]) for _ in range(2)]
        acc_t = [None, None]
        sc = sb([P, 8])
        modc = sb([P, 16])
        t_sc = act(sc[:, :], VT[:, vec["c"]:vec["c"] + 8], ACT.Silu, t_vt)
        t_gb = K.dma("scalar", "g2", G2[:, :], g["norm2_g"].partition_broadcast(P).rearrange("p a d -> p (a d)"))
        t_g1 = [None]
        t_mod = {}

        def ada_step(j, c, ten, t):
            ac = acc[j % 2]
            if c == 0 and j == 0:
                ada_start(0)
                ada_start(1)
            tp = acc_t[j % 2]
            for i in range(2):
                tp = stt(ac[:, :], ten[:, i * D:(i + 1) * D], sc[:, 2 * c + i:2 * c + i + 1], ac[:, :],
                         ALU.mult, ALU.add, tp, t, t_sc)
            acc_t[j % 2] = tp
            if c == 3 and j < 2:
                ada_end(j, ac, tp)
            elif c == 3:
                ends.append(lambda: ada_end(j, ac, tp))
            return tp

        def ada_start(j):
            ac = acc[j % 2]
            t0 = G(lambda e: e.memset(ac[:, :], 0.0), acc_t[j % 2])
            acc_t[j % 2] = K.dma("gpsimd", f"adab{j % 2}", ac[0:1, :], g["ada_b"][:, j * D:(j + 1) * D], t0)

        def ada_end(j, ac, tp):
            if j < 2:
                b = bank()
                for k in range(KC):
                    tm = mm(banks[b][:, k:k + 1], ac[:, k * P:(k + 1) * P], onesf[:, 0:1], True, True,
                            tp, t_on, bfree[b] if k == 0 else None)
                if j == 0:
                    t = V(lambda e: e.tensor_copy(modc[:, 0:8], banks[b][:, 0:8]), tm)
                else:
                    t = stt(modc[:, 8:16], banks[b][:, 0:8], 1.0, VT[:, vec["n1"]:vec["n1"] + 8],
                            ALU.add, ALU.mult, tm, t_vt)
                bfree[b] = [t]
                t_mod[j] = t
                acc_t[j % 2] = tm
                ada_start(j + 2)
                return
            for h in range(2):
                b = bank()
                hs = slice(h * 512, (h + 1) * 512)
                tm = mm(banks[b][:, :], onesf[:, :], ac[:, hs], True, True, tp, t_on, bfree[b])
                if j == 4:
                    t = stt(G2[:, hs], banks[b][:, :], 1.0, G2[:, hs], ALU.add, ALU.mult, tm, t_gb)
                else:
                    dst = {2: GA, 3: S2, 5: GF}[j]
                    t = act(dst[:, hs], banks[b][:, :], ACT.Copy, tm, t_yz if j == 5 else None)
                bfree[b] = [t]
                t_mod.setdefault(j, []).append(t)
            acc_t[j % 2] = tm
            if j < 4:
                ada_start(j + 2)

        def rstd_of(t_in):
            tr = []
            for tb in range(TB):
                t = act(XN[:, tb, :], X[:, tb, :], ACT.Square, t_in[tb], accum_out=small[:, tb:tb + 1])
                t = act(small[:, 4 + tb:5 + tb], small[:, tb:tb + 1], ACT.Sqrt, t, t_eps, scale=1.0 / D, bias=epst[:, 0:1])
                tr.append(V(lambda e, tb=tb: e.reciprocal(small[:, 8 + tb:9 + tb], small[:, 4 + tb:5 + tb]), t))
            return tr

        def normalize(t_in):
            tr = rstd_of(t_in)
            return [ts(XN[:, tb, :], X[:, tb, :], small[:, 8 + tb:9 + tb], None, ALU.mult, None, tr[tb])
                    for tb in range(TB)]

        tmp_free = [[], []]
        tmp_turn = [0]

        def to_features(hT, t_xn, gcols, scols, *t_cols):
            toks, pend = [], []

            def finish(kc, tt_, i):
                th = act(hT[0][:, kc, :], tmpT[i][:, :], ACT.Copy, tt_)
                tl = tt(hT[1][:, kc, :], tmpT[i][:, :], hT[0][:, kc, :].bitcast(F32), ALU.subtract, th)
                tmp_free[i] = [th, tl]
                toks.append([th, tl])

            for kc in range(KC):
                b = bank()
                for tb in range(TB):
                    tm = PE(lambda e, b=b, tb=tb, kc=kc: e.transpose(banks[b][:, tb * P:(tb + 1) * P],
                                                                    XN[:, tb, kc * P:(kc + 1) * P], ident[:, :]),
                            t_xn[tb], t_id, bfree[b])
                i = tmp_turn[0] % 2
                tmp_turn[0] += 1
                if gcols is None:
                    t = V(lambda e, b=b, i=i: e.tensor_copy(tmpT[i][:, :], banks[b][:, :]), tm, tmp_free[i])
                elif scols is None:
                    t = ts(tmpT[i][:, :], banks[b][:, :], gcols(kc), None, ALU.mult, None, tm, tmp_free[i], t_cols)
                else:
                    t = ts(tmpT[i][:, :], banks[b][:, :], gcols(kc), scols(kc), ALU.mult, ALU.add, tm,
                           tmp_free[i], t_cols)
                bfree[b] = [t]
                if pend:
                    finish(*pend.pop())
                pend.append((kc, t, i))
            finish(*pend.pop())
            return toks

        def t_blocks(hT, t_h, n):
            for it in range(n):
                w = take()
                bs, tms = [bank()], [None, None]
                if it == 0:
                    bs.append(bank())
                    order = [(kc, j) for kc in range(KC) for j in range(2)]
                else:
                    order = [(kc, j) for j in range(2) for kc in range(KC)]
                for kc, j in order:
                    if j == 1 and kc == 0 and it > 0:
                        yield bs[0], tms[0]
                        bs.append(bank())
                    tms[j] = mm3(banks[bs[j]][:, :], [w[i][:, kc, j * P:(j + 1) * P] for i in (0, 1)],
                                 [hT[i][:, kc, :] for i in (0, 1)], kc == 0, kc == KC - 1, w[2][kc // 4], t_h[kc],
                                 bfree[bs[j]] if kc == 0 else None)
                done(w, tms[1])
                if it == 0:
                    yield bs[0], tms[0]
                yield bs[1], tms[1]

        def n_blocks(hT, t_h, nk, k_first=0):
            bs = [bank() for _ in range(TB)]
            tms = [None] * TB
            k0, seen = k_first, 0
            while seen < nk:
                w = take()
                kn = w[0].shape[1]
                for tb in range(TB):
                    for k in range(kn):
                        tms[tb] = mm3(banks[bs[tb]][:, :], [hT[i][:, k0 + k, tb * P:(tb + 1) * P] for i in (0, 1)],
                                      [w[i][:, k, :] for i in (0, 1)], seen + k == 0, seen + k == nk - 1, w[2][2 * k // kn],
                                      t_h[k0 + k], bfree[bs[tb]] if seen + k == 0 else None)
                done(w, tms[TB - 1])
                seen += kn
                k0 = (k0 + kn) % nk
            return list(zip(bs, tms))

        def add_to_x(hT, t_h, nk, gate=None, t_gate=None, k_first=0):
            toks = [[] for _ in range(TB)]
            for h in range(2):
                hs = slice(h * 512, (h + 1) * 512)
                for tb, (b, tm) in enumerate(n_blocks(hT, t_h, nk, k_first)):
                    if gate is None:
                        t = tt(X[:, tb, hs], X[:, tb, hs], banks[b][:, :], ALU.add, tm)
                        bfree[b] = [t]
                    else:
                        i = tmp_turn[0] % 2
                        tmp_turn[0] += 1
                        t = tt(tmpT[i][:, :], banks[b][:, :], gate[:, hs], ALU.mult, tm, t_gate, tmp_free[i])
                        bfree[b] = [t]
                        t = tt(X[:, tb, hs], X[:, tb, hs], tmpT[i][:, :], ALU.add, t)
                        tmp_free[i] = [t]
                    toks[tb].append(t)
            return toks

        hTh = [sb([P, KC, T], F32R), sb([P, KC, T], F32R)]
        pump(4)
        t_xn = normalize(t_x)
        pump(4)
        prep_one(False)
        t_zy = G(lambda e: e.memset(GF[:, :], 0.0))
        t_h = to_features(hTh, t_xn, lambda kc: modc[:, 8 + kc:9 + kc], lambda kc: modc[:, kc:kc + 1],
                          t_mod[0], t_mod[1])
        UC = [XN[:, 0, 0:512], XN[:, 0, 512:1024], XN[:, 1, 0:512], XN[:, 1, 512:1024]]
        SO = [XN[:, 2, 0:512], XN[:, 2, 512:1024], XN[:, 3, 0:512], XN[:, 3, 512:1024]]
        VN = sb([P, TB, 512])
        RM = sb([4, 2, 512])
        UP = [sb([P, 515]) for _ in range(2)]
        CY = [sb([P, 512]) for _ in range(2)]
        WQ = sb([P, 3, 4, P])
        t_wq = [K.dma("scalar", "wq", WQ[:, 0, :, :], g["w_q"][0].rearrange("h d e -> d h e")),
                K.dma("scalar", "wq", WQ[:, 1, :, :], g["w_k"][0].rearrange("h d e -> d h e")),
                K.dma("scalar", "wq", WQ[:, 2, :, :], g["w_pool"][0].rearrange("h d e -> d h e"))]
        push()
        PT = sb([P, 4, 528])
        AR = [sb([P, KC * 36], F32R) for _ in range(2)]
        WIF = sb([P, KC, 8])
        WIh = [a[:, :].rearrange("p (c n) -> p c n", c=KC) for a in AR]
        t_wif = K.dma("gpsimd", "wif", WIF[:, :, :], w_in.rearrange("(c p) n -> p c n", p=P)[:, :, 1536:1544])
        tz = [V(lambda e, z=z: e.memset(z[:, :].bitcast(F32), 0.0)) for z in AR]
        t_wi = []
        for j in range(2):
            s = WIh[0][:, :, 32 * j:32 * j + 4]
            th = act(s, WIF[:, :, 4 * j:4 * j + 4], ACT.Copy, t_wif, tz)
            tl = tt(WIh[1][:, :, 32 * j:32 * j + 4], WIF[:, :, 4 * j:4 * j + 4], s.bitcast(F32), ALU.subtract,
                    th, tz, t_wif)
            t_wi += [th, tl]
        BIF = sb([4, 2])
        t_bif = [K.dma("scalar", "bif", BIF[:, 0:1], g["b_igate"].rearrange("a h -> h a")),
                 K.dma("scalar", "bif", BIF[:, 1:2], g["b_fgate"].rearrange("a h -> h a"))]
        for n in range(NE, NBLK):
            t_yz = K.dma("gpsimd", "yz", y_d[n * CAP:(n + 1) * CAP, :], GF[:, :], t_zy)
        cy_free = [None, None]
        t_uc = []
        for cb, (b, tm) in enumerate(t_blocks(hTh, t_h, 2)):
            t = act(UC[cb], banks[b][:, :], ACT.Copy, tm)
            bfree[b] = [t]
            t_uc.append(t)

        def conv(cb):
            i = cb % 2
            t = ts(CY[i][:, :], UC[cb], col("cw", 12 + cb), col("cb", cb), ALU.mult, ALU.add, t_uc[cb], t_vt, cy_free[i])
            for k in range(3):
                t = stt(CY[i][:, 3 - k:512], UC[cb][:, 0:509 + k], col("cw", 4 * k + cb), CY[i][:, 3 - k:512],
                        ALU.mult, ALU.add, t)
            cy_free[i] = t_uc[cb] = act(UC[cb], CY[i][:, :], ACT.Silu, t)

        b = bank()
        for kc in range(KC):
            tm = mm3(banks[b][0:36, :], [WIh[i][:, kc, :] for i in (0, 1)], [hTh[i][:, kc, :] for i in (0, 1)],
                     kc == 0, kc == KC - 1, t_wi, t_h[kc], bfree[b] if kc == 0 else None)
        t_if = tm
        R = [UP[0][0:4, 3:515], UP[1][0:4, 3:515], RM[:, 0, :], RM[:, 1, :]]
        t_i = ts(R[0], banks[b][0:4, :], BIF[:, 0:1], None, ALU.add, None, tm, t_bif)
        t_f = ts(R[1], banks[b][32:36, :], BIF[:, 1:2], None, ALU.add, None, tm, t_bif)
        bfree[b] = [t_i, t_f]
        t = act(R[2], R[1], ACT.Abs, t_f)
        t = act(R[2], R[2], ACT.Exp, t, scale=-1.0)
        t = act(R[2], R[2], ACT.Ln, t, t_on, bias=onesf[0:4, 0:1])
        t = stt(R[1], R[1], 0.0, R[2], ALU.min, ALU.subtract, t)
        tz = V(lambda e: e.memset(R[2], 0.0), t)
        t_b = V(lambda e: e.tensor_tensor_scan(R[3], R[1], R[2], 0.0, ALU.add, ALU.add), t, tz)
        t_r = tt(R[0], R[0], R[3], ALU.subtract, t_b, t_i)
        t = V(lambda e: e.tensor_tensor_scan(R[2], R[0], R[0], 0.0, ALU.max, ALU.max), t_r)
        t_nm = stt(R[3], R[3], -1.0, R[2], ALU.mult, ALU.subtract, t)
        t_nM = ts(R[2], R[2], -1.0, None, ALU.mult, None, t_nm)
        b = bank()
        for tb in range(TB):
            tm = PE(lambda e, b=b, tb=tb: e.transpose(banks[b][:, 4 * tb:4 * tb + 4], R[0][:, tb * P:(tb + 1) * P],
                                                     ident[0:4, 0:4]), t_r, bfree[b])
        rcol = small[:, 16:32]
        t_rc = V(lambda e, b=b: e.tensor_copy(rcol, banks[b][:, 0:16]), tm)
        bfree[b] = [t_rc]

        t_pz = V(lambda e: e.memset(PT[:, :, 0:16], 0.0))
        t_pt = []
        for gi, (b, tm) in enumerate(t_blocks(hTh, t_h, 2)):
            t = act(PT[:, gi, 16:528], banks[b][:, :], ACT.Copy, tm)
            bfree[b] = [t]
            t_pt.append(t)
            conv(gi)
        t_v = []
        for tb, (b, tm) in enumerate(n_blocks(hTh, t_h, KC)):
            t = act(VN[:, tb, :], banks[b][:, :], ACT.Copy, tm)
            bfree[b] = [t]
            t_v.append(t)
        RC = sb([P, 16])
        RI = sb([P, 16], I32)
        t0 = G(lambda e: e.iota(RI[:, :], pattern=[[1, 16]], base=1, channel_multiplier=0))
        t0 = V(lambda e: e.tensor_copy(RC[:, :], RI[:, :]), t0)
        t_rcn = V(lambda e: e.reciprocal(RC[:, :], RC[:, :]), t0)
        mix_toks = [None] * KC
        PA_ = [sb([P, 528]), sb([P, 528])]
        pfree = [cy_free[0], cy_free[1]]
        pa_tok = None
        t_yp = []
        for gi in range(4):
            src, t = PT[:, gi, :], [t_pt[gi], t_pz]
            sh = 1
            for s in range(gi + 1):
                dst = PA_[s % 2]
                lo = 2 * sh - 1
                t = gtt(dst[:, lo:528], src[:, lo:528], src[:, lo - sh:528 - sh], ALU.add, t, pa_tok)
                src = dst
                sh *= 2
            Wn = 2 ** (gi + 1)
            pw = CY[gi % 2]
            t1 = ts(pw[:, :], src[:, 16:528], 1.0 / Wn, None, ALU.mult, None, t, pfree[gi % 2])
            t2 = tt(pw[:, 0:Wn], src[:, 16:16 + Wn], RC[:, 0:Wn], ALU.mult, t, t1, t_rcn)
            pa_tok = t2
            t3 = tt(pw[:, :], pw[:, :], PT[:, gi, 16:528], ALU.subtract, t2)
            b = bank()
            tm = mm(banks[b][:, :], WQ[:, 2, gi, :], pw[:, :], True, True, t_wq, t3, bfree[b])
            pfree[gi % 2] = tm
            t = ts(PT[:, gi, 16:528], banks[b][:, :], col("bp", gi), col("psc", gi), ALU.add, ALU.mult, tm, t)
            bfree[b] = [t]
            t_yp.append(t)
        QK = [[sb([P, T]) for _ in range(2)] for _ in range(2)]
        DG = [z[:, 0:T] for z in PA_]
        EM = tmpT
        EE = [z[:, 0:T] for z in UP]
        ee_free = [[t_rc], [t_b]]
        ee_turn = [0]
        hd = [{"qk": t_if, "dg": pa_tok, "done": pfree[0]}, {"qk": t_if, "dg": pa_tok, "done": pfree[1]}]
        t_so = [None] * 4
        t_hh = [None] * 4

        def head_a(h):
            z = h % 2
            o = hd[z]
            bq, bk, bm, bn_, bd = bank(), bank(), bank(), bank(), bank()
            tqm = mm(banks[bq][:, :], WQ[:, 0, h, :], UC[h], True, True, t_wq, t_uc[h], bfree[bq])
            tkm = mm(banks[bk][:, :], WQ[:, 1, h, :], UC[h], True, True, bfree[bk])
            tq = act(QK[z][0][:, :], banks[bq][:, :], ACT.Copy, tqm, o.get("qk"), scale=float(P) ** -0.5)
            bfree[bq] = [tq]
            tk = V(lambda e: e.tensor_copy(QK[z][1][:, :], banks[bk][:, :]), tkm, o.get("qk"))
            bfree[bk] = [tk]
            tm = mm(banks[bm][:, :], sel[:, h * P:(h + 1) * P], RM[:, 0, :], True, True, t_nM, t_sel, bfree[bm])
            t_dg = tt(DG[z][:, :].rearrange("p (a c) -> p a c", a=4), banks[bm][:, :].rearrange("p (a c) -> p a c", a=4),
                      neg[:, :].unsqueeze(1).broadcast_to([P, 4, P]), ALU.add, tm, t_neg, o.get("dg"))
            t_bm = [t_dg]
            bs = {}

            def s_mm(s):
                bs[s] = bank()
                return mm(banks[bs[s]][:, 0:T - s * P], QK[z][1][:, s * P:(s + 1) * P], QK[z][0][:, s * P:T],
                          True, True, tq, tk, bfree[bs[s]])

            tms = {0: s_mm(0)}
            for s in range(TB):
                y = ee_turn[0] % 2
                ee_turn[0] += 1
                n = T - s * P
                cs = slice(s * P, T)
                if s < 3:
                    tms[s + 1] = s_mm(s + 1)
                rc = small[:, 16 + 4 * s + h:17 + 4 * s + h]
                te = [act(EE[y][:, 0:P], DG[z][:, s * P:(s + 1) * P], ACT.Exp, t_dg, t_rc, ee_free[y], bias=rc)]
                if n > P:
                    te.append(act(EE[y][:, P:n], banks[bm][:, (s + 1) * P:T], ACT.Exp, t_dg, t_rc, ee_free[y], bias=rc))
                if s == 2:
                    bfree[bm] = [te[-1]]
                t = tt(EE[y][:, 0:n], EE[y][:, 0:n], banks[bs[s]][:, 0:n], ALU.mult, tms[s], te)
                bfree[bs[s]] = [t]
                o["tn"] = mm(banks[bn_][:, cs], VN[:, s, h * P:(h + 1) * P], EE[y][:, 0:n], s == 0, s == 3, t_v, t,
                             bfree[bn_] if s == 0 else None)
                o["td"] = mm(banks[bd][:, cs], onesf[:, :], EE[y][:, 0:n], s == 0, s == 3,
                             bfree[bd] if s == 0 else None)
                ee_free[y] = [o["td"]]
            o["qk"] = tms[3]
            b = bank()
            tm = mm(banks[b][:, :], sel[:, h * P:(h + 1) * P], RM[:, 1, :], True, True, t_nm, t_sel, bfree[b])
            o["em"] = act(EM[z][:, :], banks[b][:, :], ACT.Exp, tm, o.get("done"), tmp_free[z])
            bfree[b] = [o["em"]]
            o["bn"], o["bd"] = bn_, bd

        def head_b(h):
            z = h % 2
            o = hd[z]
            bn_, bd = o["bn"], o["bd"]
            em, hh, dg = EM[z][:, :], CY[z][:, :], DG[z][:, :]
            t = act(dg, banks[bd][:, :], ACT.Abs, o["td"])
            bfree[bd] = [t]
            t = tt(em, em, dg, ALU.max, t, o["em"])
            t = V(lambda e: e.reciprocal(em, em), t)
            t = tt(hh, banks[bn_][:, :], em, ALU.mult, t, o["tn"], o.get("done"))
            bfree[bn_] = [t]
            t1 = act(dg, hh, ACT.Square, t)
            b = bank()
            tm = mm(banks[b][:, :], onesf[:, :], dg, True, True, t1, bfree[b])
            o["dg"] = tm
            t1 = act(em, banks[b][:, :], ACT.Sqrt, tm, scale=1.0 / P, bias=epst[:, 0:1])
            bfree[b] = [t1]
            t1 = V(lambda e: e.reciprocal(em, em), t1)
            t = stt(hh, hh, col("mn", h), em, ALU.mult, ALU.mult, t, t1)
            t = stt(hh, UC[h], col("sk", h), hh, ALU.mult, ALU.add, t)
            t_hh[h] = tt(UC[h], hh, SO[h], ALU.mult, t, t_so[h])
            o["done"] = t_hh[h]
            tmp_free[z] = [t_hh[h]]

        ob = t_blocks(hTh, t_h, 2)
        for h in range(4):
            head_a(h)
            b, tm = next(ob)
            t_so[h] = act(SO[h], banks[b][:, :], ACT.Sigmoid, tm)
            bfree[b] = [t_so[h]]
            if h > 0:
                head_b(h - 1)
        t_hfree = [tm]
        mixT = hTh
        for gi in range(4):
            mix_toks[4 + gi] = split(mixT[0][:, 4 + gi, :], mixT[1][:, 4 + gi, :], PT[:, gi, 16:528], t_yp[gi], t_hfree)
        for h in range(3):
            mix_toks[h] = split(mixT[0][:, h, :], mixT[1][:, h, :], UC[h], t_hh[h], t_hfree)
        head_b(3)
        mix_toks[3] = split(mixT[0][:, 3, :], mixT[1][:, 3, :], UC[3], t_hh[3], t_hfree)
        t_x = add_to_x(mixT, mix_toks, KC, GA, t_mod[2], k_first=4)
        pop()

        tr = rstd_of(t_x)
        toks = []
        for tb in range(TB):
            t = stt(XN[:, tb, :], X[:, tb, :], small[:, 8 + tb:9 + tb], G2[:, :], ALU.mult, ALU.mult, tr[tb], t_mod[4])
            t = tt(XN[:, tb, :], XN[:, tb, :], S2[:, :], ALU.add, t, t_mod[3])
            toks.append(t)
        t_xd = K.dma("scalar", "xnd", xn_d.rearrange("(t p) d -> p t d", p=P), XN[:, :, :], toks)
        t_h = to_features(hTh, toks, None, None)
        push()
        WR = sb([P, KC, 36])
        LT = sb([36, T])
        WRs = [sb([P, KC, 36], F32R), sb([P, KC, 36], F32R)]
        t_wr = [K.dma("scalar", "wr", WR[:, :, 0:4], g["w_router_group"][0].rearrange("(c p) n -> p c n", p=P)),
                K.dma("scalar", "wr", WR[:, :, 4:36], g["w_router_expert"][0].rearrange("(c p) n -> p c n", p=P)),
                K.dma("scalar", "wr", RB[:, 0:4], g["b_router_group"].partition_broadcast(P).rearrange("p a d -> p (a d)")),
                K.dma("scalar", "wr", RB[:, 4:36], g["b_router_expert"].partition_broadcast(P).rearrange("p a d -> p (a d)"))]
        ZT = sb([NBLK, P])
        t = V(lambda e: e.memset(ZT[:, :], 0.0))
        t_z = K.dma("scalar", "zt", st_d.rearrange("(b s) o -> b (s o)", s=CAP), ZT[:, :], t)
        t_ws = split(WRs[0][:, :, :], WRs[1][:, :, :], WR[:, :, :], t_wr)
        b = bank()
        for kc in range(KC):
            tm = mm3(banks[b][0:36, :], [WRs[i][:, kc, :] for i in (0, 1)], [hTh[i][:, kc, :] for i in (0, 1)],
                     kc == 0, kc == KC - 1, t_h[kc], t_ws, bfree[b])
        t = V(lambda e, b=b: e.tensor_copy(LT[:, :], banks[b][0:36, :]), tm)
        bfree[b] = [t]
        b = bank()
        for tb in range(TB):
            tm = PE(lambda e, b=b, tb=tb: e.transpose(banks[b][:, tb * 36:(tb + 1) * 36], LT[:, tb * P:(tb + 1) * P],
                                                     ident[0:36, 0:36]), t, bfree[b])
        LG = sb([P, TB, 36])
        t_lg = tt(LG[:, :, :], banks[b][:, 0:144].rearrange("p (t n) -> p t n", t=TB),
                  RB[:, :].unsqueeze(1).broadcast_to([P, TB, 36]), ALU.add, tm)
        bfree[b] = [t_lg]
        CI = sb([P, 72], I32)
        CJ = sb([P, 72])
        t0 = [G(lambda e: e.iota(CI[:, 0:4], pattern=[[-1, 4]], base=4, channel_multiplier=0)),
              G(lambda e: e.iota(CI[:, 4:36], pattern=[[-1, 32]], base=32, channel_multiplier=0)),
              G(lambda e: e.iota(CI[:, 36:68], pattern=[[1, 32]], base=0, channel_multiplier=0)),
              G(lambda e: e.iota(CI[:, 68:72], pattern=[[P, 4]], base=0, channel_multiplier=1))]
        t_cj = V(lambda e: e.tensor_copy(CJ[:, :], CI[:, :]), t0)
        EJ = CJ[:, 36:68]

        def red(out_, in_, op, *a):
            return V(lambda e: e.tensor_reduce(out_, in_, AX, op), *a)

        def bc(x, n):
            return x.unsqueeze(2).broadcast_to([P, TB, n])

        def bt(x, n):
            return x.unsqueeze(1).broadcast_to([P, TB, n])

        S = sb([P, 24, TB])
        sx = lambda i: S[:, i, :]
        W4 = sb([P, TB, 4])
        OG = sb([P, TB, 4])
        LE = sb([P, TB, 32])
        W32 = sb([P, TB, 32])
        OH = [sb([P, TB, 32]) for _ in range(2)]
        AA = sb([P, TB, 32])
        gl = LG[:, :, 0:4]
        t = red(sx(0), gl, ALU.max, t_lg)
        t1 = tt(W4[:, :, :], gl, bc(sx(0), 4), ALU.is_equal, t)
        t1 = tt(W4[:, :, :], W4[:, :, :], bt(CJ[:, 0:4], 4), ALU.mult, t1, t_cj)
        t1 = red(sx(1), W4[:, :, :], ALU.max, t1)
        t_og = tt(OG[:, :, :], W4[:, :, :], bc(sx(1), 4), ALU.is_equal, t1)
        t1 = tt(W4[:, :, :], gl, bc(sx(0), 4), ALU.subtract, t_og)
        t1 = act(W4[:, :, :], W4[:, :, :], ACT.Exp, t1)
        t1 = red(sx(2), W4[:, :, :], ALU.add, t1)
        t_pg = V(lambda e: e.reciprocal(sx(3), sx(2)), t1)
        t = ts(OG[:, :, :], OG[:, :, :], -1.0, BIG, ALU.add, ALU.mult, t_og)
        t_le = None
        for tb in range(TB):
            t_le = tt(LE[:, tb, :].rearrange("p (a c) -> p a c", a=4), LG[:, tb, 4:36].rearrange("p (a c) -> p a c", a=4),
                      OG[:, tb, :].unsqueeze(2).broadcast_to([P, 4, 8]), ALU.add, t, t_lg)
        tv = []
        t = t_le
        for k in range(2):
            t = red(sx(4 + k), LE[:, :, :], ALU.max, t)
            t = tt(W32[:, :, :], LE[:, :, :], bc(sx(4 + k), 32), ALU.is_equal, t)
            t = tt(W32[:, :, :], W32[:, :, :], bt(CJ[:, 4:36], 32), ALU.mult, t)
            t = red(sx(6), W32[:, :, :], ALU.max, t)
            t = tt(OH[k][:, :, :], W32[:, :, :], bc(sx(6), 32), ALU.is_equal, t)
            if k == 0:
                t = stt(LE[:, :, :], OH[0][:, :, :], -2.0 * BIG, LE[:, :, :], ALU.mult, ALU.add, t)
        t_oh = t
        t = tt(sx(7), sx(5), sx(4), ALU.subtract, t_oh)
        t = act(sx(7), sx(7), ACT.Exp, t)
        t1 = ts(sx(8), sx(7), 1.0, None, ALU.add, None, t)
        t1 = V(lambda e: e.reciprocal(sx(8), sx(8)), t1)
        GT = sb([P, 2, TB])
        t1 = tt(small[:, 32:36], sx(8), sx(3), ALU.mult, t1, t_pg)
        t_gt = tt(small[:, 36:40], small[:, 32:36], sx(7), ALU.mult, t1)
        t_a = tt(AA[:, :, :], OH[0][:, :, :], OH[1][:, :, :], ALU.add, t_oh)
        b = bank()
        for tb in range(TB):
            for s in range(tb + 1):
                tm = mm(banks[b][:, tb * 32:(tb + 1) * 32], tri[:, :] if s == tb else onesf[:, :], AA[:, s, :],
                        s == 0, s == tb, t_a, t_tri, bfree[b])
        for s in range(TB):
            tm = mm(banks[b][:, 128:160], onesf[:, :], AA[:, s, :], s == 0, s == 3)
        RK = sb([P, 160])
        t_rk = V(lambda e, b=b: e.tensor_copy(RK[:, :], banks[b][:, 0:160]), tm)
        bfree[b] = [t_rk]
        CN = RK[:, 128:160]
        NO = sb([P, 5, 32])
        t = ts(NO[:, 0, :], CN, float(CAP), None, ALU.is_gt, None, t_rk)
        t = stt(NO[:, 0, :], CN, 2.0 * CAP, NO[:, 0, :], ALU.is_gt, ALU.add, t)
        t = stt(NO[:, 0, :], CN, 3.0 * CAP, NO[:, 0, :], ALU.is_gt, ALU.add, t)
        tz = V(lambda e: e.memset(NO[:, 4, :], 0.0))
        t_in = V(lambda e: e.tensor_tensor_scan(NO[:, 1, :], NO[:, 0, :], NO[:, 4, :], 0.0, ALU.add, ALU.add), t, tz)
        t_bs = tt(NO[:, 2, :], NO[:, 1, :], NO[:, 0, :], ALU.subtract, t_in)
        t = tt(NO[:, 3, :], NO[:, 2, :], EJ, ALU.subtract, t_bs)
        t_of = ts(NO[:, 3, :], NO[:, 3, :], float(CAP), float((NE - 1) * CAP), ALU.mult, ALU.add, t)
        SF = sb([P, 2, TB])
        t_sl = []
        for k in range(2):
            t = None
            for i, m in enumerate((RK[:, 0:128].rearrange("p (t n) -> p t n", t=TB), bt(EJ, 32), bt(NO[:, 3, :], 32))):
                t = tt(W32[:, :, :], OH[k][:, :, :], m, ALU.mult, t_oh, t_rk, t_of, t, t_sl)
                t = red(sx(9 + i), W32[:, :, :], ALU.add, t)
            t = stt(sx(12), sx(9), float(CAP), sx(11), ALU.is_ge, ALU.mult, t)
            t = stt(sx(13), sx(10), float(CAP), sx(9), ALU.mult, ALU.add, t)
            t_sl.append(tt(SF[:, k, :], sx(12), sx(13), ALU.add, t))
        SL = SLK
        t_sli = V(lambda e: e.tensor_copy(SL[:, :, :], SF[:, :, :]), t_sl)
        t_st = []
        for k in range(2):
            for tb in range(TB):
                t_st.append(K.gather("st", st_d, SL[:, k, tb:tb + 1], CJ[:, 68 + tb:69 + tb], None, t_sli, t_z))
        IE = sb([1, NOVF, 32])
        IF_ = sb([1, NOVF, 32])
        CV = sb([1, 8])
        t_cv = []
        for n in range(NOVF):
            t = ts(IE[:, n, :], NO[0:1, 1, :], float(n), None, ALU.is_gt, None, t_in)
            t = stt(IE[:, n, :], NO[0:1, 2, :], float(n), IE[:, n, :], ALU.is_le, ALU.mult, t, t_bs)
            t_cv.append(tt(IF_[:, n, :], IE[:, n, :], CJ[0:1, 36:68], ALU.mult, t))
        t = red(CV[:, 0:NOVF], IF_[:, :, :], ALU.add, t_cv)
        t = ts(CV[:, 7:8], NO[0:1, 1, 31:32], -1.0, float(NOVF), ALU.mult, ALU.add, t)
        t_ct = V(lambda e: e.tensor_copy(CT[:, :], CV[:, :]), t)
        TT_ = sb([NBLK, P])
        t = K.dma("sync", "tt", TT_[:, :], st_d.rearrange("(b s) o -> b (s o)", s=CAP), t_st)
        b = bank()
        tm = PE(lambda e, b=b: e.transpose(banks[b][:, 0:NBLK], TT_[:, :], ident[0:NBLK, 0:NBLK]), t, bfree[b])
        t_tok = V(lambda e, b=b: e.tensor_copy(TOK[:, :], banks[b][:, 0:NBLK]), tm)
        bfree[b] = [t_tok]
        pop()
        ft = pop()
        add_raw(1, ft)
        add_split(2, ft)

        push()
        XT = [[sb([P, KC, P], F32R), sb([P, KC, P], F32R)] for _ in range(2)]
        SG = [sb([P, DE]) for _ in range(2)]
        GM = sb([P, DE])
        GTs = [sb([P, TB, P], F32R), sb([P, TB, P], F32R)]
        YB = [sb([P, D]) for _ in range(2)]
        xg_free = [[t_xd] for _ in range(4)]
        xt_free = [[], []]
        sg_free = [[], []]
        gm_free, gt_free = [], []
        yb_free = [[], []]
        t_xg = {}

        def fetch(n):
            if n < NE and n not in t_xg:
                t_xg[n] = K.gather(f"xg{n % 4}", XN[:, n % 4, :], None, xn_d, TOK[:, n:n + 1],
                                   t_tok, t_xd, xg_free[n % 4], ft)

        def turn_x(n):
            z = n % 2
            toks = []
            for half in range(2):
                b = bank()
                for k in range(4):
                    kc = 4 * half + k
                    tm = PE(lambda e, b=b, k=k, kc=kc, n=n: e.transpose(banks[b][:, k * P:(k + 1) * P],
                                                                       XN[:, n % 4, kc * P:(kc + 1) * P],
                                                                       ident[:, :]), t_xg[n], bfree[b])
                v = banks[b][:, :].rearrange("p (c n) -> p c n", c=4)
                hi, lo = (XT[z][i][:, 4 * half:4 * half + 4, :] for i in (0, 1))
                th = act(hi, v, ACT.Copy, tm, xt_free[z])
                tl = tt(lo, v, hi.bitcast(F32), ALU.subtract, th, xt_free[z])
                bfree[b] = [tl]
                toks += [th, tl]
            xg_free[n % 4] = [tm]
            return toks

        for n in range(3):
            fetch(n)
        t_xt = {0: turn_x(0)}
        t_yd = []

        def rows_in(n):
            b = bank()
            for q in range(2):
                w = take()
                for k in range(4):
                    kc = 4 * q + k
                    tm = mm3(banks[b][:, :], [XT[n % 2][i][:, kc, :] for i in (0, 1)], [w[i][:, k, :] for i in (0, 1)],
                             kc == 0, kc == KC - 1, w[2][k // 2], t_xt[n], bfree[b] if kc == 0 else None)
                done(w, tm)
            return b, tm

        def rows_out(n):
            z = n % 2
            by = [bank(), bank()]
            ty = [None, None]
            for q in range(2):
                w = take()
                for hh in range(2):
                    for k in range(2):
                        kc = 2 * q + k
                        ty[hh] = mm3(banks[by[hh]][:, :], [GTs[i][:, kc, :] for i in (0, 1)],
                                     [w[i][:, k, hh * 512:(hh + 1) * 512] for i in (0, 1)],
                                     kc == 0, kc == 3, w[2][k], t_gt[0], bfree[by[hh]] if kc == 0 else None)
                done(w, ty[1])
            gt_free[:] = [ty[1]]
            tc = []
            for hh in range(2):
                hs = slice(hh * 512, (hh + 1) * 512)
                t = act(YB[z][:, hs], banks[by[hh]][:, :], ACT.Copy, ty[hh], yb_free[z])
                bfree[by[hh]] = [t]
                tc.append(t)
            t = K.dma("scalar", f"yd{z}", y_d[n * CAP:(n + 1) * CAP, :], YB[z][:, :], tc)
            yb_free[z] = [t]

        t_gate = t_gt
        t_gt = [None]
        for n in range(NE):
            z = n % 2
            fetch(n + 3)
            b, tm = rows_in(n)
            t_sg = act(SG[z][:, :], banks[b][:, :], ACT.Silu, tm, sg_free[z])
            bfree[b] = [t_sg]
            if n > 0:
                rows_out(n - 1)
            b, tm = rows_in(n)
            xt_free[z] = [tm]
            t_gm = tt(GM[:, :], SG[z][:, :], banks[b][:, :], ALU.mult, tm, t_sg, gm_free)
            bfree[b] = [t_gm]
            sg_free[z] = [t_gm]
            if n + 1 < NE:
                t_xt[n + 1] = turn_x(n + 1)
            b = bank()
            for k in range(4):
                tm = PE(lambda e, b=b, k=k: e.transpose(banks[b][:, k * P:(k + 1) * P], GM[:, k * P:(k + 1) * P],
                                                       ident[:, :]), t_gm, bfree[b])
            gm_free = [tm]
            t_gt[0] = split(GTs[0][:, :, :], GTs[1][:, :, :], banks[b][:, :].rearrange("p (c n) -> p c n", c=4),
                            tm, gt_free)
            bfree[b] = [t_gt[0]]
        rows_out(NE - 1)
        t_gt = t_gate
        t_yd = [yb_free[0], yb_free[1]]
        ft = pop()

        push()
        RWt = [sb([P, 4, DE]) for _ in range(2)]
        XO = sb([P, KC, P])
        SO_ = sb([P, DE])
        GO = sb([P, TB, P])
        YO = sb([P, D])
        before = dict(K.last)
        for n in range(NOVF):
            K.enter(CT[0:1, 7:8], NOVF - n, t_ct, ft, t_yz, t_yd)
            if n == 0:
                K.part = "more"
                rw_t = [None, None]
                wn = 0
                t_y = None
                prev = {}
            t_xgo = K.gather("xgo", XN[:, 0, :], None, xn_d, TOK[:, NE + n:NE + n + 1], t_tok, prev.get("xt"))
            t = None
            for half in range(2):
                for k in range(4):
                    kc = 4 * half + k
                    tm = PE(lambda e, k=k, kc=kc, half=half: e.transpose(banks[half][:, k * P:(k + 1) * P],
                                                                        XN[:, 0, kc * P:(kc + 1) * P],
                                                                        ident[:, :]), t_xgo, prev.get("xe"))
            t_xe = []
            for half in range(2):
                v = banks[half][:, :].rearrange("p (c n) -> p c n", c=4)
                t_xe.append(V(lambda e, v=v, half=half: e.tensor_copy(XO[:, 4 * half:4 * half + 4, :], v),
                              tm, prev.get("ab")))
            prev["xt"], prev["xe"] = tm, t_xe
            for m in range(2):
                for q in range(2):
                    i = wn % 2
                    wn += 1
                    tw = K.dma_from("more_w%d" % i, RWt[i][:, :, :], n,
                                    lambda v, m=m, q=q: g[("w_expert_gate", "w_expert_up")[m]][0][bass.ds(v, 1), :, :]
                                    .rearrange("a (c p) n -> p (a c) n", p=P)[:, 4 * q:4 * q + 4, :], rw_t[i])
                    for k in range(4):
                        kc = 4 * q + k
                        tm = mm(banks[2 + m][:, :], XO[:, kc, :], RWt[i][:, k, :], kc == 0, kc == KC - 1,
                                tw, t_xe, prev.get("g") if kc == 0 else None)
                    rw_t[i] = tm
            prev["ab"] = tm
            t = act(SO_[:, :], banks[2][:, :], ACT.Silu, tm, prev.get("gt"))
            t = tt(SO_[:, :], SO_[:, :], banks[3][:, :], ALU.mult, t, tm)
            prev["g"] = t
            for k in range(4):
                tm = PE(lambda e, k=k: e.transpose(banks[4][:, k * P:(k + 1) * P], SO_[:, k * P:(k + 1) * P],
                                                  ident[:, :]), t, prev.get("go"))
            prev["gt"] = tm
            t_go = V(lambda e: e.tensor_copy(GO[:, :, :], banks[4][:, :].rearrange("p (c n) -> p c n", c=4)),
                     tm, prev.get("dn"))
            prev["go"] = t_go
            for q in range(2):
                i = wn % 2
                wn += 1
                tw = K.dma_from("more_w%d" % i, RWt[i][:, :, :].rearrange("p (a b) n -> p a (b n)", a=2), n,
                                lambda v, q=q: g["w_expert_down"][0][bass.ds(v, 1), :, :]
                                .rearrange("a (c p) n -> p (a c) n", p=P)[:, 2 * q:2 * q + 2, :], rw_t[i])
                for hh in range(2):
                    for k in range(2):
                        kc = 2 * q + k
                        tm = mm(banks[5 + hh][:, :], GO[:, kc, :], RWt[i][:, 2 * k + hh, :], kc == 0, kc == 3,
                                tw, t_go, prev.get("yo") if kc == 0 else None)
                rw_t[i] = tm
            prev["dn"] = tm
            tc = [V(lambda e, hh=hh: e.tensor_copy(YO[:, hh * 512:(hh + 1) * 512], banks[5 + hh][:, :]), tm, t_y)
                  for hh in range(2)]
            prev["yo"] = tc
            t_y = K.dma("scalar", "more_y", y_d[(NE + n) * CAP:(NE + n + 1) * CAP, :], YO[:, :], tc)
            for e in K.q:
                K.wait(e, t_y)
        for n in range(NOVF):
            K.leave()
        K.part = "main"
        K.last = before
        t_join = A(lambda e: e.activation(small[:, 40:41], small[:, 32:33], ACT.Copy), t_gt)
        ft = [pop(), t_join]

        push()
        FGb = sb([P, D])
        Y2 = [[sb([P, D]), sb([P, D])] for _ in range(2)]
        t_fg = K.dma("scalar", "fg", FGb[:, :], g["final_g"].partition_broadcast(P), ft)
        y_free = [[ft], [ft]]
        t_x = []
        for tb in range(TB):
            z = tb % 2
            ty = [K.gather(f"y{z}{k}", Y2[z][k][:, :], None, y_d, SLK[:, k, tb:tb + 1], t_yd, t_join, y_free[z])
                  for k in range(2)]
            t = ts(Y2[z][0][:, :], Y2[z][0][:, :], small[:, 32 + tb:33 + tb], None, ALU.mult, None, ty, t_gt)
            t = stt(Y2[z][0][:, :], Y2[z][1][:, :], small[:, 36 + tb:37 + tb], Y2[z][0][:, :], ALU.mult, ALU.add, t)
            t = tt(Y2[z][0][:, :], Y2[z][0][:, :], GF[:, :], ALU.mult, t, t_mod[5])
            t = tt(X[:, tb, :], X[:, tb, :], Y2[z][0][:, :], ALU.add, t)
            y_free[z] = [t]
            t_x.append([t])
        t_xn = normalize(t_x)
        t_x = [tt(X[:, tb, :], XN[:, tb, :], FGb[:, :], ALU.mult, t_xn[tb], t_fg) for tb in range(TB)]
        pop()

        push()
        UT = sb([P, KC, T])
        BSP = GF[:, :].rearrange("p (g t) -> p g t", g=8)
        WSN = [z[:, :].rearrange("p (g s) -> p g s", g=4) for z in tmpT]
        WS = sb([P, 8, P])
        t_bsp = K.dma("scalar", "bsp", GF[:, :],
                      g["a_b_sp_2"][0].rearrange("g t -> (g t)").partition_broadcast(P), ft, t_x)
        t_ws = []
        for q in range(2):
            t = K.dma("scalar", f"wsn{q}", WSN[q], g["a_w_sp_2"][0, 4 * q:4 * q + 4].rearrange("g t s -> t g s"),
                      ft, tmp_free[q])
            t = G(lambda e, q=q: e.affine_select(out=WSN[q], in_=WSN[q], compare_op=ALU.is_ge, fill=0.0,
                                                 base=0, pattern=[[0, 4], [-1, P]], channel_multiplier=1), t)
            b = bank()
            for k in range(4):
                tm = PE(lambda e, b=b, k=k, q=q: e.transpose(banks[b][:, k * P:(k + 1) * P], WSN[q][:, k, :],
                                                            ident[:, :]), t, bfree[b])
            tmp_free[q] = [tm]
            v = banks[b][:, :].rearrange("p (c n) -> p c n", c=4)
            t = act(WS[:, 4 * q:4 * q + 4, :], v, ACT.Copy, tm)
            bfree[b] = [t]
            t_ws.append(t)
        push()
        hTh = [sb([P, KC, T], F32R), sb([P, KC, T], F32R)]
        t_xn = normalize(t_x)
        t_h = to_features(hTh, t_xn, lambda kc: col("an", kc), None)
        t_v = [[] for _ in range(TB)]
        for h in range(2):
            for tb, (b, tm) in enumerate(n_blocks(hTh, t_h, KC)):
                t = act(XN[:, tb, h * 512:(h + 1) * 512], banks[b][:, :], ACT.Gelu_apprx_tanh, tm, t_h,
                        accum_out=small[:, 2 * tb + h:2 * tb + h + 1])
                bfree[b] = [t]
                t_v[tb].append(t)
        for tb in range(TB):
            mu, sq, rs = (small[:, k + tb:k + tb + 1] for k in (8, 12, 44))
            t = tt(mu, small[:, 2 * tb:2 * tb + 1], small[:, 2 * tb + 1:2 * tb + 2], ALU.add, t_v[tb])
            t = ts(mu, mu, -1.0 / D, None, ALU.mult, None, t)
            tq = []
            for h in range(2):
                tq.append(act(tmpT[h][:, :], XN[:, tb, h * 512:(h + 1) * 512], ACT.Square, t, tmp_free[h], bias=mu,
                              accum_out=small[:, 2 * tb + h:2 * tb + h + 1]))
                tmp_free[h] = [tq[h]]
            t = tt(sq, small[:, 2 * tb:2 * tb + 1], small[:, 2 * tb + 1:2 * tb + 2], ALU.add, tq)
            t = act(sq, sq, ACT.Sqrt, t, scale=1.0 / D, bias=epst[:, 0:1])
            t = V(lambda e, rs=rs, sq=sq: e.reciprocal(rs, sq), t)
            t_v[tb] = ts(XN[:, tb, :], XN[:, tb, :], mu, rs, ALU.add, ALU.mult, t)
        t_u = []
        for gi, (b, tm) in enumerate(t_blocks(hTh, t_h, 4)):
            t = act(UT[:, gi, :], banks[b][:, :], ACT.Gelu_apprx_tanh, tm)
            bfree[b] = [t]
            b = bank()
            for tb in range(TB):
                tz = mm(banks[b][:, tb * P:(tb + 1) * P], XN[:, tb, gi * P:(gi + 1) * P], WS[:, gi, :], True, True,
                        t_v[tb], t_ws, bfree[b])
            i = tmp_turn[0] % 2
            tmp_turn[0] += 1
            t1 = stt(tmpT[i][:, :].rearrange("p (a c) -> p a c", a=4), banks[b][:, :].rearrange("p (a c) -> p a c", a=4),
                     col("av", gi), BSP[:, gi, :].unsqueeze(1).broadcast_to([P, 4, P]), ALU.mult, ALU.add,
                     tz, t_bsp, tmp_free[i])
            bfree[b] = [t1]
            t = tt(UT[:, gi, :], tmpT[i][:, :], UT[:, gi, :], ALU.mult, t, t1)
            tmp_free[i] = [t]
            t_u.append(t)
        mixT = hTh
        toks = [split(mixT[0][:, gi, :], mixT[1][:, gi, :], UT[:, gi, :], t_u[gi], tm) for gi in range(8)]
        t_x = add_to_x(mixT, toks, KC)
        pop()
        pop()

        def ffn(l, t_x):
            push()
            hTh = [sb([P, KC, T], F32R), sb([P, KC, T], F32R)]
            AT = [sb([P, 8, T], F32R), sb([P, 8, T], F32R)]
            SB_ = tmpT
            t_xn = normalize(t_x)
            t_h = to_features(hTh, t_xn, lambda kc: col("fn", 8 * l + kc), None)
            at_free = []
            sb_free = tmp_free
            t_x = None
            for f0, fn in FG:
                toks = []
                for f in range(0, fn, 2):
                    gs = []
                    for j, (b, tm) in enumerate(t_blocks(hTh, t_h, 1)):
                        t = act(SB_[j][:, :], banks[b][:, :], ACT.Silu, tm, sb_free[j])
                        bfree[b] = [t]
                        gs.append(t)
                    for j, (b, tm) in enumerate(t_blocks(hTh, t_h, 1)):
                        t = tt(SB_[j][:, :], SB_[j][:, :], banks[b][:, :], ALU.mult, tm, gs[j])
                        bfree[b] = [t]
                        sb_free[j] = split(AT[0][:, f + j, :], AT[1][:, f + j, :], SB_[j][:, :], t, at_free)
                        toks.append(sb_free[j])
                t_x = add_to_x(AT, toks, fn)
                at_free = [K.last["tensor"]]
            pop()
            return t_x

        t_x = ffn(0, t_x)

        push()
        QO = sb([P, 8, T])
        KF = sb([P, 8, T])
        push()
        hTh = [sb([P, KC, T], F32R), sb([P, KC, T], F32R)]
        t_xn = normalize(t_x)
        t_h = to_features(hTh, t_xn, lambda kc: col("bn", kc), None)
        t_q = []
        for i, (b, tm) in enumerate(t_blocks(hTh, t_h, 4)):
            t = act(QO[:, i, :], banks[b][:, :], ACT.Copy, tm)
            bfree[b] = [t]
            t_q.append(t)
        K.wait("scalar", tm)
        K.wait("vector", tm)
        t_h = to_features(hTh, t_xn, lambda kc: col("kvn", kc), None)
        t_v = []
        for h in range(2):
            for tb, (b, tm) in enumerate(n_blocks(hTh, t_h, KC)):
                t = act(XN[:, tb, h * 512:(h + 1) * 512], banks[b][:, :], ACT.Copy, tm, t_h)
                bfree[b] = [t]
                t_v.append(t)
        t_k = []
        for i, (b, tm) in enumerate(t_blocks(hTh, t_h, 4)):
            t = act(KF[:, i, :], banks[b][:, :], ACT.Copy, tm)
            bfree[b] = [t]
            t_k.append(t)
        pop()
        push()
        LAM = tmpT[0][:, 0:256].rearrange("p (a d) -> p a d", a=4)
        AB, NDf = GF[:, 0:T], GF[:, T:D]
        P1 = sb([P, 1280])
        PP = [[sb([P, 1280]), P1] for _ in range(2)]
        AT = [sb([P, T]) for _ in range(2)]
        ST = sb([P, 2, 4, 2, TB])
        NDi = PP[0][0][:, 0:T].bitcast(I32)
        t_lm = K.dma("scalar", "lam", tmpT[0][:, 0:256],
                     g["b_lambda_2"][0].rearrange("a d -> (a d)").partition_broadcast(P), tmp_free[0])
        ls = small[:, 48:56]
        t = tt(LAM[:, 0, :], LAM[:, 0, :], LAM[:, 1, :], ALU.mult, t_lm)
        t = tt(LAM[:, 2, :], LAM[:, 2, :], LAM[:, 3, :], ALU.mult, t)
        t = V(lambda e: e.tensor_reduce(ls[:, 0:1], LAM[:, 0, :], AX, ALU.add), t)
        t = V(lambda e: e.tensor_reduce(ls[:, 1:2], LAM[:, 2, :], AX, ALU.add), t)
        tmp_free[0] = [t]
        t = act(ls[:, 2:4], ls[:, 0:2], ACT.Exp, t)
        t = tt(ls[:, 4:5], ls[:, 3:4], ls[:, 2:3], ALU.subtract, t)
        t_nl = ts(ls[:, 5:6], ls[:, 4:5], -LAMBDA_INIT, None, ALU.add, None, t)
        t_sb = ts(ls[:, 6:7], col("sub", 0), 1.0 - LAMBDA_INIT, None, ALU.mult, None, t_vt)
        t = G(lambda e: e.iota(NDi, pattern=[[1, T]], base=-384, channel_multiplier=-1))
        t = V(lambda e: e.tensor_copy(NDf, NDi), t)
        t_nd = G(lambda e: e.affine_select(out=NDf, in_=NDf, compare_op=ALU.is_ge, fill=-BIG, base=384,
                                           pattern=[[-1, T]], channel_multiplier=1), t)
        off = [0, 128, 384, 768]
        pp_free, p1_free = [[t_nd], [t_nd]], []
        ab_free, at_free = [], [[], []]
        at_turn = [0]
        st_free = [[], []]
        hd = [{} for _ in range(8)]

        def scores(h):
            nonlocal ab_free
            z = h % 2
            o = hd[h]
            slope = 2.0 ** (-(h + 1))
            t_ab = ts(AB, NDf, slope * 8.0, None, ALU.mult, None, t_nd, ab_free)
            o["e"] = [[], []]
            for tb in range(TB):
                n = (tb + 1) * P
                for m in range(2):
                    pr = slice(64 * m, 64 * m + 64)
                    pt = PP[z][m][:, off[tb]:off[tb] + n]
                    b = bank()
                    tm = mm(banks[b][:, 0:n], QO[pr, h, tb * P:(tb + 1) * P], KF[pr, h, 0:n], True, True,
                            t_q[h], t_k[h], bfree[b])
                    mx, ng, sm_ = (ST[:, z, i, m, tb:tb + 1] for i in range(3))
                    t = V(lambda e, b=b, pt=pt, n=n, tb=tb, mx=mx: e.tensor_tensor_reduce(
                        out=pt, in0=banks[b][:, 0:n], in1=AB[:, 384 - tb * P:512], scale=1.0, scalar=-3.0e38,
                        op0=ALU.add, op1=ALU.max, accum_out=mx), tm, t_ab,
                        p1_free if m else pp_free[z], st_free[z])
                    bfree[b] = [t]
                    ab_free = [t]
                    t = ts(ng, mx, -0.125, None, ALU.mult, None, t)
                    t = act(pt, pt, ACT.Exp, t, scale=0.125, bias=ng, accum_out=sm_)
                    o["e"][m].append(t)

        def combine(h):
            z = h % 2
            o = hd[h]
            rr = ST[:, z, 3, :, :]
            tr = V(lambda e: e.reciprocal(rr, ST[:, z, 2, :, :]), o["e"])
            t1 = tt(ST[:, z, 3, 1, :], ST[:, z, 3, 1, :], ls[:, 5:6].broadcast_to([P, TB]), ALU.mult, tr, t_nl)
            o["a"] = []
            for tb in range(TB):
                n = (tb + 1) * P
                a0, a1 = (PP[z][m][:, off[tb]:off[tb] + n] for m in (0, 1))
                t = act(a0, a0, ACT.Copy, tr, scale=ST[:, z, 3, 0, tb:tb + 1])
                o["a"].append(stt(a0, a1, ST[:, z, 3, 1, tb:tb + 1], a0, ALU.mult, ALU.add, t, t1))
            st_free[z] = o["a"]
            p1_free[:] = o["a"]

        def values(h):
            z = h % 2
            o = hd[h]
            pend = []
            bo = bank()

            def turn(s):
                n = T - s * P
                b = bank()
                for tb in range(s, TB):
                    tm = PE(lambda e, tb=tb: e.transpose(
                        banks[b][:, (tb - s) * P:(tb - s + 1) * P],
                        PP[z][0][:, off[tb] + s * P:off[tb] + (s + 1) * P], ident[:, :]), o["a"][tb], bfree[b])
                y = at_turn[0] % 2
                at_turn[0] += 1
                t = act(AT[y][:, 0:n], banks[b][:, 0:n], ACT.Copy, tm, at_free[y])
                bfree[b] = [t]
                if s == 3:
                    pp_free[z] = [tm]
                return y, t

            nxt = turn(0)
            for s in range(TB):
                y, t = nxt
                if s < 3:
                    nxt = turn(s + 1)
                tm = mm(banks[bo][:, s * P:T], XN[:, s, h * P:(h + 1) * P], AT[y][:, 0:T - s * P],
                        s == 0, s == 3, t_v, t, bfree[bo] if s == 0 else None)
                at_free[y] = [tm]
            o["bo"], o["pv"] = bo, tm

        def tail1(h):
            o = hd[h]
            i = h % 2
            bo = o["bo"]
            o["o"] = V(lambda e: e.tensor_copy(QO[:, h, :], banks[bo][:, :]), o["pv"])
            o["sq"] = act(tmpT[i][:, :], QO[:, h, :], ACT.Square, o["o"], tmp_free[i])
            bfree[bo] = [o["o"]]

        def tail2(h):
            o = hd[h]
            i = h % 2
            b = bank()
            tm = mm(banks[b][:, :], onesf[:, :], tmpT[i][:, :], True, True, o["sq"], bfree[b])
            t = act(tmpT[i][:, :], banks[b][:, :], ACT.Sqrt, tm, scale=1.0 / P, bias=epst[:, 0:1])
            bfree[b] = [t]
            t = V(lambda e: e.reciprocal(tmpT[i][:, :], tmpT[i][:, :]), t)
            t = stt(QO[:, h, :], QO[:, h, :], ls[:, 6:7], tmpT[i][:, :], ALU.mult, ALU.mult, t, t_sb, o["o"])
            tmp_free[i] = [t]
            t_o.append(t)

        t_o = []
        for h in range(10):
            if h < 8:
                scores(h)
            if h in (3, 5, 7, 9):
                tail2(h - 3)
                tail2(h - 2)
            if 1 <= h < 9:
                values(h - 1)
            if h < 8:
                combine(h)
            if 1 <= h < 9:
                tail1(h - 1)
        pop()
        push()
        mixT = [sb([P, KC, T], F32R), sb([P, KC, T], F32R)]
        toks = [split(mixT[0][:, h, :], mixT[1][:, h, :], QO[:, h, :], t_o[h]) for h in range(8)]
        t_x = add_to_x(mixT, toks, KC)
        pop()
        pop()
        t_x = ffn(1, t_x)
        push()
        FGb = sb([P, D])
        t_fg = K.dma("scalar", "fg", FGb[:, :], g["final_norm_2"].partition_broadcast(P), K.last["scalar"])
        t_xn = normalize(t_x)
        t_x = [tt(X[:, tb, :], XN[:, tb, :], FGb[:, :], ALU.mult, t_xn[tb], t_fg) for tb in range(TB)]
        finish_x(t_x)


_INS = ['x', 'c', 'ada_w', 'ada_b', 'norm1_g', 'w_in', 'conv_w', 'conv_b', 'w_q', 'w_k', 'b_igate', 'b_fgate',
        'mlstm_norm_g', 'mlstm_skip', 'w_pool', 'b_pool', 'pool_scale', 'w_out', 'norm2_g', 'w_router_group',
        'b_router_group', 'w_router_expert', 'b_router_expert', 'w_expert_gate', 'w_expert_up', 'w_expert_down',
        'final_g', 'a_norm_2', 'a_w_in_2', 'a_v_norm_2', 'a_w_sp_2', 'a_b_sp_2', 'a_w_out_2', 'ffn_norm_2',
        'ffn_w_gu_2', 'ffn_w_down_2', 'kv_norm_2', 'kv_w_2', 'b_norm_2', 'b_w_q_2', 'b_lambda_2', 'b_subln_2',
        'b_w_o_2', 'final_norm_2']


def kernel(**inputs):
    import numpy as np
    import concourse.bacc as bacc
    from concourse.bass_utils import run_bass_kernel_spmd

    nc = bacc.Bacc("TRN2", target_bir_lowering=False, num_devices=1)
    arrays, g = {}, {}
    for name in _INS:
        a = np.ascontiguousarray(inputs[name])
        arrays[f"in_{name}"] = a
        g[name] = nc.dram_tensor(f"in_{name}", a.shape, mybir.dt.from_np(a.dtype), kind="ExternalInput").ap()
    out = nc.dram_tensor("out_x", (1, T, D), F32, kind="ExternalOutput").ap()
    program(nc, g, out)
    r = run_bass_kernel_spmd(nc, [arrays], core_ids=[0])
    return r.results[0]["out_x"]
```
